# Optimizing a Trainium2 kernel written in Bass

```python
import jax, jax.numpy as jnp
from jax import lax
import numpy as np

D_MODEL = 2048
BATCH = 1
SEQ = 512
DEPTH = 1

CHUNK = 64
MIX_WIDTH = D_MODEL
HG_HEADS = 8
HG_HEAD_DIM = 128
HG_WIDTH = HG_HEADS * HG_HEAD_DIM
ATT_HEADS = 8
ATT_HEAD_DIM = 128
ATT_WIDTH = ATT_HEADS * ATT_HEAD_DIM
LEFT_CHUNKS = 8
BAND = (LEFT_CHUNKS + 1) * CHUNK
REL_CLIP = 128
D_FF = 5632
CONV_WIDTH = 3
PLE_DIM = 256
EPS = 1e-6
IN_SPLITS = (HG_WIDTH, HG_WIDTH, HG_WIDTH, HG_WIDTH, ATT_WIDTH, ATT_WIDTH, ATT_WIDTH)
IN_COLS = sum(IN_SPLITS)

kernel_name = "hybrid_hgrn2_chunkattn_convffn_ple"

def rmsnorm(x, g):
    xf = x.astype(jnp.float32)
    y = xf * lax.rsqrt(jnp.mean(xf * xf, axis=-1, keepdims=True) + EPS)
    return (y * g.astype(jnp.float32)).astype(x.dtype)

def hgrn2_mixer(q, f_pre, i_in, g, lb, norm_g):
    B, S, _ = q.shape
    nc = S // CHUNK
    lb = lb.astype(jnp.float32)
    sig = jax.nn.sigmoid(f_pre.astype(jnp.float32))
    f = lb + (1.0 - lb) * sig
    log_f = jnp.log(f)
    k = (1.0 - lb) * jax.nn.sigmoid(-f_pre.astype(jnp.float32))
    qf = jax.nn.silu(q.astype(jnp.float32))
    vf = i_in.astype(jnp.float32)

    def heads(t):
        return t.reshape(B, nc, CHUNK, HG_HEADS, HG_HEAD_DIM).transpose(1, 0, 3, 2, 4)

    causal = jnp.tril(jnp.ones((CHUNK, CHUNK), dtype=bool))

    def step(state, inp):
        qc, kc, vc, lfc = inp
        b = jnp.cumsum(lfc, axis=2)
        diff = b[:, :, :, None, :] - b[:, :, None, :, :]
        decay = jnp.exp(jnp.where(causal[None, None, :, :, None], diff, -jnp.inf))
        scores = jnp.einsum('bhtd,bhsd,bhtsd->bhts', qc, kc, decay)
        o_intra = jnp.einsum('bhts,bhsv->bhtv', scores, vc)
        o_inter = jnp.einsum('bhtd,bhdv->bhtv', qc * jnp.exp(b), state)
        b_last = b[:, :, -1:, :]
        new_state = (jnp.exp(b_last[:, :, 0, :])[..., None] * state
                     + jnp.einsum('bhsd,bhsv->bhdv', kc * jnp.exp(b_last - b), vc))
        return new_state, o_intra + o_inter

    s0 = jnp.zeros((B, HG_HEADS, HG_HEAD_DIM, HG_HEAD_DIM), jnp.float32)
    _, o = lax.scan(step, s0, (heads(qf), heads(k), heads(vf), heads(log_f)))
    o = o.transpose(1, 0, 3, 2, 4).reshape(B, S, HG_HEADS, HG_HEAD_DIM)
    o = rmsnorm(o, norm_g)
    gate = jax.nn.silu(g.astype(jnp.float32)).reshape(B, S, HG_HEADS, HG_HEAD_DIM)
    return (o * gate).reshape(B, S, HG_WIDTH).astype(q.dtype)

def chunk_attention(q, k, v, rel_bias):
    B, S, _ = q.shape
    nc = S // CHUNK
    pad = LEFT_CHUNKS * CHUNK

    def heads(t):
        return t.reshape(B, S, ATT_HEADS, ATT_HEAD_DIM).transpose(0, 2, 1, 3)

    qh = heads(q) * (ATT_HEAD_DIM ** -0.5)
    kp = jnp.pad(heads(k), ((0, 0), (0, 0), (pad, 0), (0, 0)))
    vp = jnp.pad(heads(v), ((0, 0), (0, 0), (pad, 0), (0, 0)))
    t_off = jnp.arange(CHUNK)[:, None]
    j_off = jnp.arange(BAND)[None, :]
    rel = t_off + pad - j_off
    bias = rel_bias.astype(jnp.float32)[:, jnp.clip(rel, -REL_CLIP, REL_CLIP) + REL_CLIP]
    band_idx = jnp.arange(BAND)

    def one_chunk(c):
        start = c * CHUNK
        qc = lax.dynamic_slice_in_dim(qh, start, CHUNK, axis=2)
        kc = lax.dynamic_slice_in_dim(kp, start, BAND, axis=2)
        vc = lax.dynamic_slice_in_dim(vp, start, BAND, axis=2)
        s = jnp.einsum('bhtd,bhsd->bhts', qc, kc).astype(jnp.float32) + bias[None]
        valid = (start - pad + band_idx) >= 0
        s = jnp.where(valid[None, None, None, :], s, jnp.finfo(jnp.float32).min)
        pr = jax.nn.softmax(s, axis=-1)
        return jnp.einsum('bhts,bhsd->bhtd', pr.astype(vc.dtype), vc)

    out = lax.map(one_chunk, jnp.arange(nc))
    return out.transpose(1, 0, 3, 2, 4).reshape(B, S, ATT_WIDTH)

def conv_ffn(h, w_up, conv_w, conv_b, w_down):
    S = h.shape[1]
    u = h @ w_up
    up = jnp.pad(u, ((0, 0), (CONV_WIDTH - 1, 0), (0, 0)))
    uc = conv_b + sum(conv_w[j] * up[:, j:j + S] for j in range(CONV_WIDTH))
    gate, val = uc[..., :D_FF], uc[..., D_FF:]
    return (jax.nn.silu(gate) * val) @ w_down

def setup_inputs(seed: int = 0) -> dict:
    key = jax.random.key(seed)
    ks = jax.random.split(key, 20)
    f32 = jnp.float32
    nrm = lambda k, shape, s: jax.random.normal(k, shape, f32) * s
    return {
        "x": nrm(ks[0], (BATCH, SEQ, D_MODEL), 1.0),
        "p": nrm(ks[1], (DEPTH, BATCH, SEQ, PLE_DIM), 1.0),
        "norm_mix": 1.0 + nrm(ks[2], (DEPTH, D_MODEL), 0.02),
        "w_in": nrm(ks[3], (DEPTH, D_MODEL, IN_COLS), D_MODEL ** -0.5),
        "lb_logits": nrm(ks[4], (DEPTH + 1, HG_WIDTH), 0.5),
        "hg_norm": 1.0 + nrm(ks[5], (DEPTH, HG_HEAD_DIM), 0.02),
        "rel_bias": nrm(ks[6], (DEPTH, ATT_HEADS, 2 * REL_CLIP + 1), 0.5),
        "w_out": nrm(ks[7], (DEPTH, MIX_WIDTH, D_MODEL), MIX_WIDTH ** -0.5),
        "norm_ffn": 1.0 + nrm(ks[8], (DEPTH, D_MODEL), 0.02),
        "w_up": nrm(ks[9], (DEPTH, D_MODEL, 2 * D_FF), D_MODEL ** -0.5),
        "conv_w": nrm(ks[10], (DEPTH, CONV_WIDTH, 2 * D_FF), CONV_WIDTH ** -0.5),
        "conv_b": nrm(ks[11], (DEPTH, 2 * D_FF), 0.02),
        "w_down": nrm(ks[12], (DEPTH, D_FF, D_MODEL), D_FF ** -0.5),
        "norm_ple": 1.0 + nrm(ks[13], (DEPTH, D_MODEL), 0.02),
        "w_ple_gate": nrm(ks[14], (DEPTH, D_MODEL, D_MODEL), D_MODEL ** -0.5),
        "w_ple_proj": nrm(ks[15], (DEPTH, PLE_DIM, D_MODEL), PLE_DIM ** -0.5),
        "final_norm": 1.0 + nrm(ks[16], (D_MODEL,), 0.02),
    }

def reference(x, p, norm_mix, w_in, lb_logits, hg_norm, rel_bias, w_out, norm_ffn,
              w_up, conv_w, conv_b, w_down, norm_ple, w_ple_gate, w_ple_proj, final_norm):
    lb_all = jnp.cumsum(jax.nn.softmax(lb_logits.astype(jnp.float32), axis=0), axis=0)[:DEPTH]
    split_idx = [int(v) for v in np.cumsum(IN_SPLITS)[:-1]]
    h = x
    for i in range(DEPTH):
        a = rmsnorm(h, norm_mix[i])
        proj = a @ w_in[i]
        hq, hf, hi, hg, aq, ak, av = jnp.split(proj, split_idx, axis=-1)
        y_hg = hgrn2_mixer(hq, hf, hi, hg, lb_all[i], hg_norm[i])
        y_att = chunk_attention(aq, ak, av, rel_bias[i])
        h = h + jnp.concatenate([y_hg, y_att], axis=-1) @ w_out[i]
        h = h + conv_ffn(rmsnorm(h, norm_ffn[i]), w_up[i], conv_w[i], conv_b[i], w_down[i])
        gate = jax.nn.sigmoid(rmsnorm(h, norm_ple[i]) @ w_ple_gate[i])
        h = h + gate * (p[i] @ w_ple_proj[i])
    return rmsnorm(h, final_norm)


_drawn_inputs = setup_inputs


def setup_inputs(seed=0):
    import zlib

    import numpy as np

    out = dict(_drawn_inputs(seed))
    spreads = {}
    factors = {'norm_mix': 4.549,
     'hg_norm': 5.919,
     'norm_ffn': 12.469,
     'conv_b': 12.382,
     'norm_ple': 200.0,
     'final_norm': 24.528,
     'p': 8.0,
     'w_ple_gate': 8.0,
     'w_ple_proj': 8.0}
    for name, (base, spread) in spreads.items():
        noise = np.random.default_rng([zlib.crc32(name.encode()), seed]).standard_normal(out[name].shape)
        drawn = base * np.exp(spread * noise) if base else spread * noise
        out[name] = __import__('jax').numpy.asarray(drawn.astype(out[name].dtype))
    for name, factor in factors.items():
        out[name] = (out[name] * factor).astype(out[name].dtype)
    return out
```

```python
from contextlib import ExitStack

import concourse.bass as bass
from concourse import mybir

F32 = mybir.dt.float32
F32R = mybir.dt.float32r
U32 = mybir.dt.uint32
ALU = mybir.AluOpType
ACT = mybir.ActivationFunctionType
AX = mybir.AxisListType

P = 128
S = 512
D = 2048
KT = D // P
HEADS = 8
NJ = 7
UK = 8
FFT = 5632 // P
GROUPS = 4
FG = FFT // GROUPS
PK = 2
CT = S // P
LEVELS = 8
EPS = 1e-6
LOWEST = -3.3895314e38
SU = 2 * NJ

U_OUT = HEADS * SU
U_FFN = U_OUT + 2 * KT
U_GRP = 4 * FG + KT
U_PLE = U_FFN + GROUPS * U_GRP
U_END = U_PLE + 3 * KT
T_OUT = HEADS * NJ
T_FFN = T_OUT + KT
T_GRP = 2 * FG + KT
T_PLE = T_FFN + GROUPS * T_GRP


def level_offset(m):
    return 1024 - 1024 // m


def build(nc, xT, gains, w_in, lb_logits, hg_gain, bias_rows, w_out, w_up, conv, w_down,
          w_gate, w_proj, pT, masks, eye, outT):
    with ExitStack() as ctx:
        def sb(name, shape, dt=F32):
            return ctx.enter_context(nc.sbuf_tensor(name, shape, dt))

        def sem(name):
            return ctx.enter_context(nc.semaphore(name))

        raw = [sb(f"raw{i}", [P, FG * P]) for i in range(2)]
        w_hi = [sb(f"w_hi{i}", [P, FG * P], F32R) for i in range(2)]
        w_lo = [sb(f"w_lo{i}", [P, FG * P], F32R) for i in range(2)]
        rstd = sb("rstd", [P, S])
        root = sb("root", [P, S])
        sq_sum = sb("sq_sum", [P, S])
        sq = [sb(f"sq{i}", [P, S]) for i in range(2)]
        gain = sb("gain", [P, 4, KT])
        conv_c = sb("conv_c", [P, 2 * FFT, 4])
        ones = sb("ones", [P, P])
        ident = sb("ident", [P, P])
        lbl = sb("lbl", [P, 2, HEADS])
        lb = sb("lb", [P, 6, HEADS])
        lb_now = sb("lb_now", [P, 2])
        hgn = sb("hgn", [P, 1])
        bias_now = sb("bias_now", [P, 1])
        eps = sb("eps", [P, 1])
        neg_max = sb("neg_max", [P, 2])
        row_sum = sb("row_sum", [P, 2])
        row_inv = sb("row_inv", [P, 2])

        base = (nc.sbuf_base + 63) // 64 * 64
        R1, R2, RH = base, base + 65536, base + 131072

        def at(name, off, shape, dt=F32):
            return nc.alloc_sbuf_tensor_at(name, shape, dt, offset=off)

        a_hi = at("a_hi", R1, [P, KT, S], F32R)
        a_lo = at("a_lo", R1 + 32768, [P, KT, S], F32R)
        y_hi = at("y_hi", R1, [P, KT, S], F32R)
        y_lo = at("y_lo", R1 + 32768, [P, KT, S], F32R)
        f_hi = at("f_hi", R1, [P, FG, S], F32R)
        f_lo = at("f_lo", R1 + 22528, [P, FG, S], F32R)
        o = R1 + 45056
        u_gate = at("u_gate", o, [P, 520]); o += 2080
        u_val = at("u_val", o, [P, 520]); o += 2080
        c_gate = at("c_gate", o, [P, S]); o += 2048
        c_val = at("c_val", o, [P, S]); o += 2048
        s_gate = at("s_gate", o, [P, S]); o += 2048
        f_act = at("f_act", o, [P, S]); o += 2048
        p_raw = at("p_raw", R1, [P, PK, S])
        p_hi = at("p_hi", R1 + 4096, [P, PK, S], F32R)
        p_lo = at("p_lo", R1 + 8192, [P, PK, S], F32R)
        g_pre = [at(f"g_pre{i}", R1 + 12288 + 2048 * i, [P, S]) for i in range(2)]
        g_sig = [at(f"g_sig{i}", R1 + 16384 + 2048 * i, [P, S]) for i in range(2)]
        y = at("y", R2, [P, KT, S])
        o = R2 + 32768
        stage = [at(f"stage{j}", o + 2048 * j, [P, S]) for j in range(NJ)]; o += 2048 * NJ
        v_hg = at("v_hg", o, [P, CT, P]); o += 2048
        v_att = at("v_att", o, [P, CT, P]); o += 2048
        prob_t = at("prob_t", o, [P, CT, S]); o += 8192
        intra = at("intra", o, [P, CT, P]); o += 2048
        mask = at("mask", o, [P, LEVELS, P]); o += 4096
        assert o <= RH
        n_hi = at("n_hi", R2, [P, KT, S], F32R)
        n_lo = at("n_lo", R2 + 32768, [P, KT, S], F32R)
        result = at("result", R2, [P, KT, S])
        h = at("h", RH, [P, KT, S])
        o = RH
        q = at("q", o, [P, S]); o += 2048
        k = at("k", o, [P, S]); o += 2048
        fg = at("fg", o, [P, 1024]); o += 4096
        gate = at("gate", o, [P, S]); o += 2048
        og = at("og", o, [P, S]); o += 2048
        o_sq = at("o_sq", o, [P, S]); o += 2048
        o_rs = at("o_rs", o, [P, S]); o += 2048
        k_tok = at("k_tok", o, [P, CT, P]); o += 2048
        state = at("state", o, [P, CT - 1, P]); o += 2048
        prob = [at(f"prob{i}", o + 2048 * i, [P, S]) for i in range(2)]; o += 4096
        bias = at("bias", o, [P, HEADS, 2 * P]); o += 8192
        assert o <= RH + 32768

        pt = [ctx.enter_context(nc.psum_tensor(f"pt{i}", [P, S], F32)) for i in range(3)]
        pl = [ctx.enter_context(nc.psum_tensor(f"pl{i}", [P, S], F32)) for i in range(2)]
        px = ctx.enter_context(nc.psum_tensor("px", [P, S], F32))
        py = ctx.enter_context(nc.psum_tensor("py", [P, S], F32))
        ps = ctx.enter_context(nc.psum_tensor("ps", [P, S], F32))

        raw_in = [sem(f"raw_in{i}") for i in range(2)]
        hi_ready = sem("hi_ready")
        lo_ready = sem("lo_ready")
        unit_done = sem("unit_done")
        evac_done = sem("evac_done")
        x_in = [sem(f"x_in{i}") for i in range(4)]
        const_in = sem("const_in")
        bias_in = sem("bias_in")
        p_in = sem("p_in")
        consts = sem("consts")
        nh_ready = sem("nh_ready")
        nl_ready = sem("nl_ready")
        sq_ready = sem("sq_ready")
        sq_added = sem("sq_added")
        ms_done = sem("ms_done")
        root_ready = sem("root_ready")
        rstd_ready = sem("rstd_ready")
        h_final = sem("h_final")
        lb_step = sem("lb_step")
        lb_exp = sem("lb_exp")
        bias_cut = sem("bias_cut")
        hg_in = sem("hg_in")
        lb_set = sem("lb_set")
        hg_upd = sem("hg_upd")
        lvl_done = sem("lvl_done")
        lvl_masked = sem("lvl_masked")
        vt_done = sem("vt_done")
        v_copied = sem("v_copied")
        kt_done = sem("kt_done")
        kt_copied = sem("kt_copied")
        kv_done = sem("kv_done")
        st_step = sem("st_step")
        hg_out = sem("hg_out")
        hg_sq = sem("hg_sq")
        hg_og = sem("hg_og")
        hg_ms = sem("hg_ms")
        hg_root = sem("hg_root")
        hg_rs = sem("hg_rs")
        y_hg = sem("y_hg")
        sc_done = sem("sc_done")
        sc_read = sem("sc_read")
        sc_max = sem("sc_max")
        sc_exp = sem("sc_exp")
        sc_inv = sem("sc_inv")
        sc_prob = sem("sc_prob")
        pt_done = sem("pt_done")
        pt_copied = sem("pt_copied")
        att_out = sem("att_out")
        y_att = sem("y_att")
        yh_ready = sem("yh_ready")
        yl_ready = sem("yl_ready")
        cg_step = sem("cg_step")
        cv_step = sem("cv_step")
        down_read = sem("down_read")
        silu_done = sem("silu_done")
        fh_ready = sem("fh_ready")
        fl_ready = sem("fl_ready")
        ph_ready = sem("ph_ready")
        pl_ready = sem("pl_ready")
        gp_ready = sem("gp_ready")
        gs_ready = sem("gs_ready")
        gm_ready = sem("gm_ready")
        res_ready = sem("res_ready")
        stored = sem("stored")

        def wait(eng, s, value):
            if not (isinstance(value, int) and value <= 0):
                eng.wait_ge(s, value)

        def wait_apart(eng, s, value):
            if isinstance(value, int):
                wait(eng, s, value)
            else:
                ready = eng.snap(value)
                eng.wait_ge(consts, 1)
                eng.wait_ge(s, ready)

        block = ctx.enter_context(nc.Block())

        @block.sync
        def _(sp):
            def load(slot, src, width, freed):
                wait(sp, lo_ready, freed)
                sp.dma_start(raw[slot][:, 0:width], src).then_inc(raw_in[slot], 16)

            def load_x(i):
                sp.dma_start(h[:, 4 * i:4 * i + 4, :], xT[:, 4 * i:4 * i + 4, :]).then_inc(x_in[i], 16)

            load_x(0)
            load(0, w_in[0], UK * P, 0)
            for i in (1, 2, 3):
                load_x(i)
            load(1, w_in[1], UK * P, 0)
            with sp.Fori(1, U_OUT // 2) as i:
                load(0, w_in[2 * i], UK * P, 2 * i - 1)
                load(1, w_in[2 * i + 1], UK * P, 2 * i)
            load(0, w_out[0], UK * P, U_OUT - 1)
            load(1, w_out[1], UK * P, U_OUT)
            sp.wait_ge(y_hg, HEADS)
            sp.wait_ge(y_att, HEADS)
            for i in range(4):
                load_x(i)
            with sp.Fori(1, KT) as i:
                load(0, w_out[2 * i], UK * P, U_OUT + 2 * i - 1)
                load(1, w_out[2 * i + 1], UK * P, U_OUT + 2 * i)
            with sp.Fori(0, GROUPS) as g:
                with sp.Fori(0, 2 * FG) as i:
                    load(0, w_up[g * (4 * FG) + 2 * i], UK * P, U_FFN + U_GRP * g + 2 * i - 1)
                    load(1, w_up[g * (4 * FG) + 2 * i + 1], UK * P, U_FFN + U_GRP * g + 2 * i)
                with sp.Fori(0, KT // 2) as i:
                    load(0, w_down[g * KT + 2 * i], FG * P, U_FFN + U_GRP * g + 4 * FG + 2 * i - 1)
                    load(1, w_down[g * KT + 2 * i + 1], FG * P, U_FFN + U_GRP * g + 4 * FG + 2 * i)

            def load_gate_pair(i, first=False):
                n = U_PLE + 6 * i
                load(0, w_gate[4 * i], UK * P, n - 1)
                load(1, w_gate[4 * i + 1], UK * P, n)
                if first:
                    sp.wait_ge(unit_done, U_PLE)
                    sp.dma_start(p_raw[:], pT).then_inc(p_in, 16)
                load(0, w_proj[2 * i], PK * P, n + 1)
                load(1, w_gate[4 * i + 2], UK * P, n + 2)
                load(0, w_gate[4 * i + 3], UK * P, n + 3)
                load(1, w_proj[2 * i + 1], PK * P, n + 4)

            load_gate_pair(0, first=True)
            with sp.Fori(1, KT // 2) as i:
                load_gate_pair(i)
            for i in range(4):
                sp.wait_ge(res_ready, 4 * i + 4)
                sp.dma_start(outT[:, 4 * i:4 * i + 4, :], result[:, 4 * i:4 * i + 4, :]).then_inc(stored, 16)
            sp.wait_ge(stored, 64)

        @block.gpsimd
        def _(pool):
            nc.gpsimd.memset(ones[:], 1.0)
            nc.gpsimd.memset(eps[:], EPS).then_inc(consts, 1)
            for r in range(4):
                wait(pool, ms_done, r)
                nc.gpsimd.memset(sq_sum[:], 0.0).then_inc(sq_added, 1)
                with pool.Fori(0, KT // 2) as i:
                    for b in range(2):
                        n = r * (KT + 1) + 2 * i + b
                        pool.wait_ge(sq_ready, r * KT + 2 * i + b + 1)
                        pool.wait_ge(sq_added, n + 1)
                        nc.gpsimd.tensor_tensor(sq_sum[:], sq_sum[:], sq[b][:], ALU.add).then_inc(sq_added, 1)

        @block.scalar
        def _(act):
            def split(n, slot, width, count=None):
                act.wait_ge(raw_in[slot], 16 * count)
                wait(act, unit_done, n - 1)
                nc.scalar.activation(w_hi[slot][:, 0:width], raw[slot][:, 0:width], ACT.Copy).then_inc(hi_ready, 1)

            def norm_tile(r, m, b, dst, g):
                wait(act, sq_added, r * (KT + 1) + m)
                if dst is not None:
                    nc.scalar.activation(dst[:, bass.ds(m, 1), :], h[:, bass.ds(m, 1), :], ACT.Copy,
                                         scale=gain[:, g, bass.ds(m, 1)]).then_inc(nh_ready, 1)
                nc.scalar.activation(sq[b][:], h[:, bass.ds(m, 1), :], ACT.Square).then_inc(sq_ready, 1)

            def norm_root(r):
                act.wait_ge(ms_done, r + 1)
                nc.scalar.activation(root[:], px[:], ACT.Sqrt, bias=eps[:], scale=1.0 / D).then_inc(root_ready, 1)

            act.dma_start(gain[:], gains).then_inc(const_in, 16)
            act.dma_start(lbl[:], lb_logits).then_inc(const_in, 16)
            act.dma_start(hgn[:], hg_gain).then_inc(const_in, 16)
            act.dma_start(ident[:], eye).then_inc(const_in, 16)
            act.dma_start(mask[:], masks).then_inc(const_in, 16)
            act.dma_start(conv_c[:], conv).then_inc(const_in, 16)
            act.wait_ge(const_in, 96)
            act.wait_ge(consts, 1)
            split(0, 0, UK * P, 1)
            for m in range(KT):
                if m % 4 == 0:
                    act.wait_ge(x_in[m // 4], 16)
                norm_tile(0, m, m % 2, a_hi, 0)
                if m == 3:
                    split(1, 1, UK * P, 1)
            act.wait_ge(nl_ready, KT)
            act.wait_ge(sq_ready, KT)
            act.wait_ge(lb_step, 1)
            nc.scalar.activation(lb[:, 1:3, :], lb[:, 1:3, :], ACT.Exp).then_inc(lb_exp, 1)
            act.dma_start(bias[:], bias_rows).then_inc(bias_in, 16)

            def mix(g, s):
                if s == 0:
                    act.wait_ge(evac_done, NJ * g + NJ)
                    nc.scalar.activation(fg[:, 0:S], stage[0][:], ACT.Sigmoid)
                    nc.scalar.activation(k[:], stage[0][:], ACT.Sigmoid, scale=-1.0)
                    nc.scalar.activation(q[:], stage[1][:], ACT.Silu)
                    nc.scalar.activation(gate[:], stage[3][:], ACT.Silu).then_inc(hg_in, 1)
                if s == 1:
                    act.wait_ge(vt_done, g + 1)
                    nc.scalar.activation(v_hg[:].rearrange("p c d -> p (c d)"), px[:], ACT.Copy).then_inc(v_copied, 1)
                    nc.scalar.activation(v_att[:].rearrange("p c d -> p (c d)"), py[:], ACT.Copy).then_inc(v_copied, 1)
                if 2 <= s <= 5:
                    t = s - 2
                    act.wait_ge(pt_done, CT * g + t + 1)
                    nc.scalar.activation(prob_t[:, 0:t + 1, t * P:(t + 1) * P],
                                         py[:, 0:(t + 1) * P].rearrange("p (j t) -> p j t", t=P),
                                         ACT.Copy).then_inc(pt_copied, 1)
                if 1 <= s <= 4:
                    t = s - 1
                    act.wait_ge(sc_max, CT * g + t + 1)
                    nc.scalar.activation(prob[t % 2][:, 0:(t + 1) * P], prob[t % 2][:, 0:(t + 1) * P], ACT.Exp,
                                         bias=neg_max[:, t % 2:t % 2 + 1],
                                         accum_out=row_sum[:, t % 2:t % 2 + 1]).then_inc(sc_exp, 1)
                if s == 6:
                    act.wait_ge(att_out, g + 1)
                    nc.scalar.activation(y[:, bass.ds(2 * g + 1, 1), :], py[:], ACT.Copy).then_inc(y_att, 1)
                if s == 9:
                    act.wait_ge(kt_done, g + 1)
                    nc.scalar.activation(k_tok[:].rearrange("p c d -> p (c d)"), px[:], ACT.Copy).then_inc(kt_copied, 1)
                if s == 11:
                    act.wait_ge(hg_og, g + 1)
                    nc.scalar.activation(o_sq[:], py[:], ACT.Square).then_inc(hg_sq, 1)
                if s == 12:
                    act.wait_ge(hg_ms, g + 1)
                    nc.scalar.activation(o_rs[:], px[:], ACT.Sqrt, bias=eps[:], scale=1.0 / P).then_inc(hg_root, 1)

            def y_split(kk):
                nc.scalar.activation(y_hi[:, kk, :], y[:, kk, :], ACT.Copy).then_inc(yh_ready, 1)

            def pair(hh, proj, mixing):
                for s in range(SU):
                    if proj and not (isinstance(hh, int) and hh == 0 and s < 2):
                        split(SU * hh + s, s % 2, UK * P, NJ * hh + s // 2 + 1)
                    if s >= 1 and mixing:
                        mix(hh - 1, s - 1)
                    if not proj:
                        if s == 1:
                            split(U_OUT, 0, UK * P, U_OUT // 2 + 1)
                            split(U_OUT + 1, 1, UK * P, U_OUT // 2 + 1)
                        if s >= 1:
                            y_split(s - 1)
                    if proj and not mixing and s == 3:
                        norm_root(0)

            pair(0, True, False)
            with act.Fori(1, HEADS) as hh:
                pair(hh, True, True)
            pair(HEADS, False, True)
            act.wait_ge(y_hg, HEADS)
            for kk in range(SU - 1, KT):
                y_split(kk)

            act.wait_ge(yl_ready, KT)

            def after_h(r, m, b, g, dst):
                wait_apart(act, h_final, (r - 1) * KT + m + 1)
                norm_tile(r, m, b, dst, g)

            def out_pair(i, first):
                for b in range(2):
                    m = 2 * i + b
                    n = U_OUT + 4 * i + 2 * b
                    if not (first and b == 0):
                        split(n, 0, UK * P, U_OUT // 2 + m + 1)
                        split(n + 1, 1, UK * P, U_OUT // 2 + m + 1)
                        after_h(1, m - 1, (b + 1) % 2, 1, n_hi)

            out_pair(0, True)
            with act.Fori(1, KT // 2) as i:
                out_pair(i, False)

            def up_pair(g, i, head=None):
                n = U_FFN + U_GRP * g + 4 * i
                c = U_FFN // 2 + U_GRP // 2 * g + 2 * i
                split(n, 0, UK * P, c + 1)
                split(n + 1, 1, UK * P, c + 1)
                if head:
                    head()
                else:
                    finish_value(g, i - 1)
                split(n + 2, 0, UK * P, c + 2)
                split(n + 3, 1, UK * P, c + 2)
                act.wait_ge(cg_step, 4 * (FG * g + i) + 4)
                nc.scalar.activation(s_gate[:], c_gate[:], ACT.Silu).then_inc(silu_done, 1)

            def finish_value(g, i):
                wait_apart(act, cv_step, 5 * (FG * g + i) + 5)
                nc.scalar.activation(f_hi[:, bass.ds(i, 1), :], f_act[:], ACT.Copy).then_inc(fh_ready, 1)

            def down(g, last):
                n = U_FFN + U_GRP * g + 4 * FG
                c = (U_FFN + 4 * FG) // 2 + U_GRP // 2 * g
                split(n, 0, FG * P, c + 1)
                finish_value(g, FG - 1)
                split(n + 1, 1, FG * P, c + 1)

                def two(i):
                    for b in range(2):
                        split(n + 2 * i + b, b, FG * P, c + i + 1)
                        if last:
                            after_h(2, 2 * i + b - 2, b, 2, n_hi)
                with act.Fori(1, KT // 2) as i:
                    two(i)

            def first_ffn():
                after_h(1, KT - 1, 1, 1, n_hi)
                norm_root(1)

            up_pair(0, 0, first_ffn)
            with act.Fori(1, FG) as i:
                up_pair(0, i)
            down(0, False)
            with act.Fori(1, GROUPS - 1) as g:
                up_pair(g, 0, lambda: None)
                with act.Fori(1, FG) as i:
                    up_pair(g, i)
                down(g, False)
            up_pair(GROUPS - 1, 0, lambda: None)
            with act.Fori(1, FG) as i:
                up_pair(GROUPS - 1, i)
            down(GROUPS - 1, True)

            def sigmoid(m, b):
                act.wait_ge(gp_ready, m + 1)
                nc.scalar.activation(g_sig[b][:], g_pre[b][:], ACT.Sigmoid).then_inc(gs_ready, 1)
                after_h(3, m, b, 3, None)

            def gate_pair(i, first=False):
                n = U_PLE + 6 * i
                c = U_PLE // 2 + 3 * i
                split(n, 0, UK * P, c + 1)
                if first:
                    after_h(2, KT - 2, 0, 2, n_hi)
                split(n + 1, 1, UK * P, c + 1)
                if first:
                    after_h(2, KT - 1, 1, 2, n_hi)
                    norm_root(2)
                    act.wait_ge(p_in, 16)
                    nc.scalar.activation(p_hi[:], p_raw[:], ACT.Copy).then_inc(ph_ready, 1)
                else:
                    sigmoid(2 * i - 1, 1)
                split(n + 2, 0, PK * P, c + 2)
                split(n + 3, 1, UK * P, c + 2)
                split(n + 4, 0, UK * P, c + 3)
                sigmoid(2 * i, 0)
                split(n + 5, 1, PK * P, c + 3)

            gate_pair(0, True)
            with act.Fori(1, KT // 2) as i:
                gate_pair(i)
            sigmoid(KT - 1, 1)
            norm_root(3)

        @block.vector
        def _(dve):
            def split(n, slot, width):
                dve.wait_ge(hi_ready, n + 1)
                nc.vector.tensor_tensor(w_lo[slot][:, 0:width], raw[slot][:, 0:width],
                                        w_hi[slot][:, 0:width].bitcast(F32), ALU.subtract).then_inc(lo_ready, 1)

            def norm_low(c, m, dst, hi, g):
                dve.wait_ge(nh_ready, c + 1)
                nc.vector.scalar_tensor_tensor(dst[:, bass.ds(m, 1), :], h[:, bass.ds(m, 1), :],
                                               gain[:, g, bass.ds(m, 1)],
                                               hi[:, bass.ds(m, 1), :].bitcast(F32),
                                               ALU.mult, ALU.subtract).then_inc(nl_ready, 1)

            def norm_factor(r):
                dve.wait_ge(root_ready, r + 1)
                nc.vector.reciprocal(rstd[:], root[:]).then_inc(rstd_ready, 1)
                dve.wait_ge(rstd_ready, r + 1)

            nc.vector.memset(intra[:], 0.0).then_inc(lvl_masked, 1)
            dve.wait_ge(const_in, 96)
            split(0, 0, UK * P)
            for m in range(KT):
                norm_low(m, m, a_lo, a_hi, 0)
                if m == 3:
                    split(1, 1, UK * P)
            nc.vector.tensor_tensor(lb[:, 0, :], lbl[:, 0, :], lbl[:, 1, :], ALU.max).then_inc(lb_set, 1)
            dve.wait_ge(lb_set, 1)
            nc.vector.tensor_tensor(lb[:, 1, :], lbl[:, 0, :], lb[:, 0, :], ALU.subtract)
            nc.vector.tensor_tensor(lb[:, 2, :], lbl[:, 1, :], lb[:, 0, :], ALU.subtract).then_inc(lb_step, 1)
            dve.wait_ge(lb_exp, 1)
            nc.vector.tensor_tensor(lb[:, 3, :], lb[:, 1, :], lb[:, 2, :], ALU.add).then_inc(lb_step, 1)
            dve.wait_ge(lb_step, 2)
            nc.vector.reciprocal(lb[:, 3, :], lb[:, 3, :]).then_inc(lb_step, 1)
            dve.wait_ge(lb_step, 3)
            nc.vector.tensor_tensor(lb[:, 4, :], lb[:, 1, :], lb[:, 3, :], ALU.mult).then_inc(lb_step, 1)
            dve.wait_ge(lb_step, 4)
            nc.vector.tensor_scalar(lb[:, 5, :], lb[:, 4, :], -1.0, 1.0, ALU.mult, ALU.add).then_inc(lb_step, 1)
            dve.wait_ge(lb_step, 5)
            dve.wait_ge(bias_in, 16)
            nc.vector.memset(bias[0:64, :, P + 64:2 * P], LOWEST).then_inc(bias_cut, 1)

            def evac(hh, j):
                dve.wait_ge(unit_done, SU * hh + 2 * j + 2)
                if j in (0, 1, 3):
                    wait(dve, hg_in, hh)
                elif j == 2:
                    wait(dve, vt_done, hh)
                elif j < 6:
                    wait(dve, sc_done, CT * hh)
                nc.vector.tensor_tensor(stage[j][:], pt[2 if j == 6 else j % 2][:], rstd[:],
                                        ALU.mult).then_inc(evac_done, 1)

            def softmax_head(g, t):
                dve.wait_ge(sc_done, CT * g + t + 1)
                if t >= 2:
                    dve.wait_ge(pt_done, CT * g + t - 1)
                dst = prob[t % 2]
                scale = float(P) ** -0.5
                if t >= 2:
                    nc.vector.tensor_scalar(dst[:, 0:(t - 1) * P], ps[:, 0:(t - 1) * P], scale,
                                            bias_now[:, 0:1], ALU.mult, ALU.add)
                lo = max(t - 1, 0) * P
                nc.vector.scalar_tensor_tensor(dst[:, lo:(t + 1) * P], ps[:, lo:(t + 1) * P], scale,
                                               bias[:, bass.ds(g, 1), (P if t == 0 else 0):2 * P],
                                               ALU.mult, ALU.add).then_inc(sc_read, 1)
                dve.wait_ge(sc_read, CT * g + t + 1)
                nc.vector.tensor_reduce(neg_max[:, t % 2:t % 2 + 1], dst[:, 0:(t + 1) * P], AX.X, ALU.max,
                                        negate=True).then_inc(sc_max, 1)

            def softmax_tail(g, t):
                dve.wait_ge(sc_exp, CT * g + t + 1)
                nc.vector.reciprocal(row_inv[:, t % 2:t % 2 + 1], row_sum[:, t % 2:t % 2 + 1]).then_inc(sc_inv, 1)
                dve.wait_ge(sc_inv, CT * g + t + 1)
                nc.vector.tensor_scalar(prob[t % 2][:, 0:(t + 1) * P], prob[t % 2][:, 0:(t + 1) * P],
                                        row_inv[:, t % 2:t % 2 + 1], None, ALU.mult).then_inc(sc_prob, 1)

            def halves(buf, off, m):
                return buf[:, off:off + S].rearrange("p (b two m) -> p b two m", two=2, m=m)

            def mix(g, s):
                if 1 <= s <= 4:
                    softmax_head(g, s - 1)
                if s == 0:
                    nc.vector.tensor_copy(lb_now[:], lb[:, 4:6, bass.ds(g, 1)].rearrange("p a b -> p (a b)"))
                    nc.vector.tensor_copy(bias_now[:], bias[:, bass.ds(g, 1), 0:1].rearrange("p a b -> p (a b)")).then_inc(lb_set, 1)
                    dve.wait_ge(hg_in, g + 1)
                    dve.wait_ge(lb_set, g + 2)
                    nc.vector.tensor_scalar(k[:], k[:], lb_now[:, 1:2], None, ALU.mult)
                    nc.vector.tensor_scalar(fg[:, 0:S], fg[:, 0:S], lb_now[:, 1:2], lb_now[:, 0:1],
                                            ALU.mult, ALU.add).then_inc(hg_upd, 1)
                if 1 <= s <= LEVELS:
                    lvl = s - 1
                    dve.wait_ge(lvl_done, LEVELS * g + lvl + 1)
                    dve.wait_ge(hg_upd, 9 * g + s)
                    dve.wait_ge(lvl_masked, LEVELS * g + s)
                    if s == 1:
                        nc.vector.tensor_tensor(q[:], q[:], fg[:, 0:S], ALU.mult).then_inc(hg_upd, 1)
                    else:
                        m = 2 ** (s - 2)
                        nb = S // m
                        f_m = fg[:, level_offset(m):level_offset(m) + nb].rearrange("p (b two) -> p b two", two=2)
                        qv, kv = halves(q, 0, m), halves(k, 0, m)
                        nc.vector.tensor_tensor(qv[:, :, 1, :], qv[:, :, 1, :],
                                                f_m[:, :, 0:1].to_broadcast([P, nb // 2, m]), ALU.mult)
                        nc.vector.tensor_tensor(kv[:, :, 0, :], kv[:, :, 0, :],
                                                f_m[:, :, 1:2].to_broadcast([P, nb // 2, m]), ALU.mult)
                        nxt = level_offset(2 * m)
                        nc.vector.tensor_tensor(fg[:, nxt:nxt + nb // 2], f_m[:, :, 0], f_m[:, :, 1],
                                                ALU.mult).then_inc(hg_upd, 1)
                    nc.vector.copy_predicated(
                        intra[:], mask[:, lvl:lvl + 1, :].bitcast(U32).to_broadcast([P, CT, P]),
                        pl[lvl % 2][:].rearrange("p (c t) -> p c t", t=P)).then_inc(lvl_masked, 1)
                if s == 10:
                    dve.wait_ge(kv_done, g + 1)
                    t128 = level_offset(P)
                    nc.vector.tensor_copy(state[:, 0, :], px[:, 0:P]).then_inc(st_step, 1)
                    for c in (1, 2):
                        dve.wait_ge(st_step, 3 * g + c)
                        nc.vector.scalar_tensor_tensor(state[:, c, :], state[:, c - 1, :], fg[:, t128 + c:t128 + c + 1],
                                                       px[:, c * P:(c + 1) * P], ALU.mult, ALU.add).then_inc(st_step, 1)
                if s == 11:
                    dve.wait_ge(hg_out, g + 1)
                    nc.vector.scalar_tensor_tensor(og[:], py[:], hgn[:, 0:1], gate[:], ALU.mult, ALU.mult).then_inc(hg_og, 1)
                if s == 12:
                    dve.wait_ge(hg_root, g + 1)
                    nc.vector.reciprocal(o_rs[:], o_rs[:]).then_inc(hg_rs, 1)
                    dve.wait_ge(hg_rs, g + 1)
                    dve.wait_ge(hg_og, g + 1)
                    nc.vector.tensor_tensor(y[:, bass.ds(2 * g, 1), :], og[:], o_rs[:], ALU.mult).then_inc(y_hg, 1)
                if 1 <= s <= 4:
                    softmax_tail(g, s - 1)

            def y_split(kk):
                dve.wait_ge(yh_ready, kk + 1)
                nc.vector.tensor_tensor(y_lo[:, kk, :], y[:, kk, :], y_hi[:, kk, :].bitcast(F32),
                                        ALU.subtract).then_inc(yl_ready, 1)

            def pair(hh, proj, mixing):
                for s in range(SU):
                    if proj and s >= 3 and s % 2 == 1:
                        if not mixing and s == 3:
                            norm_factor(0)
                        evac(hh, (s - 3) // 2)
                    if mixing and s == 1:
                        evac(hh - 1, NJ - 1)
                    if proj and not (isinstance(hh, int) and hh == 0 and s < 2):
                        split(SU * hh + s, s % 2, UK * P)
                    if s >= 1 and mixing:
                        mix(hh - 1, s - 1)
                    if not proj:
                        if s == 1:
                            split(U_OUT, 0, UK * P)
                            split(U_OUT + 1, 1, UK * P)
                        if s >= 1:
                            y_split(s - 1)

            pair(0, True, False)
            with dve.Fori(1, HEADS) as hh:
                pair(hh, True, True)
            pair(HEADS, False, True)
            for kk in range(SU - 1, KT):
                y_split(kk)

            def out_tile(m, b):
                dve.wait_ge(unit_done, U_OUT + 2 * m + 2)
                nc.vector.tensor_tensor(h[:, bass.ds(m, 1), :], h[:, bass.ds(m, 1), :], pt[b][:],
                                        ALU.add).then_inc(h_final, 1)
                norm_low(KT + m, m, n_lo, n_hi, 1)

            def out_pair(i, first):
                for b in range(2):
                    m = 2 * i + b
                    n = U_OUT + 4 * i + 2 * b
                    if not (first and b == 0):
                        split(n, 0, UK * P)
                        split(n + 1, 1, UK * P)
                        out_tile(m - 1, (b + 1) % 2)

            for i in range(4):
                dve.wait_ge(x_in[i], 32)
            out_pair(0, True)
            with dve.Fori(1, KT // 2) as i:
                out_pair(i, False)

            def conv_tile(u, c, steps, count, col, bank, done):
                dve.wait_ge(unit_done, done)
                nc.vector.tensor_tensor(u[:, 2:2 + S], pt[bank][:], rstd[:], ALU.mult).then_inc(steps, 1)
                dve.wait_ge(steps, count + 1)
                nc.vector.tensor_scalar(c[:], u[:, 2:2 + S], conv_c[:, bass.ds(col, 1), 2:3],
                                        conv_c[:, bass.ds(col, 1), 3:4], ALU.mult, ALU.add).then_inc(steps, 1)
                for tap in (1, 0):
                    dve.wait_ge(steps, count + 3 - tap)
                    nc.vector.scalar_tensor_tensor(c[:], u[:, tap:tap + S], conv_c[:, bass.ds(col, 1), tap:tap + 1],
                                                   c[:], ALU.mult, ALU.add).then_inc(steps, 1)

            def gate_tile(g, i):
                t = FG * g + i
                wait(dve, silu_done, t)
                conv_tile(u_gate, c_gate, cg_step, 4 * t, 2 * t, 0, U_FFN + U_GRP * g + 4 * i + 2)

            def value_tile(g, i):
                t = FG * g + i
                conv_tile(u_val, c_val, cv_step, 5 * t, 2 * t + 1, 1, U_FFN + U_GRP * g + 4 * i + 4)
                dve.wait_ge(cv_step, 5 * t + 4)
                dve.wait_ge(silu_done, t + 1)
                nc.vector.tensor_tensor(f_act[:], s_gate[:], c_val[:], ALU.mult).then_inc(cv_step, 1)
                dve.wait_ge(fh_ready, t + 1)
                nc.vector.tensor_tensor(f_lo[:, bass.ds(i, 1), :], f_act[:], f_hi[:, bass.ds(i, 1), :].bitcast(F32),
                                        ALU.subtract).then_inc(fl_ready, 1)

            def down_tile(g, m, b, last):
                dve.wait_ge(unit_done, U_FFN + U_GRP * g + 4 * FG + m + 1)
                nc.vector.tensor_tensor(h[:, bass.ds(m, 1), :], h[:, bass.ds(m, 1), :], pt[b][:],
                                        ALU.add).then_inc(h_final if last else down_read, 1)
                if last:
                    norm_low(2 * KT + m, m, n_lo, n_hi, 2)

            def up_pair(g, i, head=None):
                n = U_FFN + U_GRP * g + 4 * i
                split(n, 0, UK * P)
                if head:
                    head(0)
                split(n + 1, 1, UK * P)
                if head:
                    head(1)
                else:
                    value_tile(g, i - 1)
                split(n + 2, 0, UK * P)
                split(n + 3, 1, UK * P)
                gate_tile(g, i)

            def down(g, last):
                n = U_FFN + U_GRP * g + 4 * FG
                split(n, 0, FG * P)
                value_tile(g, FG - 1)
                split(n + 1, 1, FG * P)
                with dve.Fori(1, KT // 2) as i:
                    for b in range(2):
                        split(n + 2 * i + b, b, FG * P)
                        down_tile(g, 2 * i + b - 2, b, last)

            def first_ffn(b):
                if b:
                    out_tile(KT - 1, 1)
                    nc.vector.memset(u_gate[:, 0:2], 0.0)
                    nc.vector.memset(u_val[:, 0:2], 0.0)
                    norm_factor(1)

            up_pair(0, 0, first_ffn)
            with dve.Fori(1, FG) as i:
                up_pair(0, i)
            down(0, False)
            with dve.Fori(1, GROUPS - 1) as g:
                up_pair(g, 0, lambda b: down_tile(g - 1, KT - 2 + b, b, False))
                with dve.Fori(1, FG) as i:
                    up_pair(g, i)
                down(g, False)
            up_pair(GROUPS - 1, 0, lambda b: down_tile(GROUPS - 2, KT - 2 + b, b, False))
            with dve.Fori(1, FG) as i:
                up_pair(GROUPS - 1, i)
            down(GROUPS - 1, True)

            def ple_tile(m, b):
                dve.wait_ge(unit_done, U_PLE + 3 * m + 3)
                nc.vector.tensor_tensor(g_pre[b][:], pt[b][:], rstd[:], ALU.mult).then_inc(gp_ready, 1)
                dve.wait_ge(gs_ready, m + 1)
                nc.vector.tensor_tensor(g_sig[b][:], g_sig[b][:], pl[b][:], ALU.mult).then_inc(gm_ready, 1)
                dve.wait_ge(gm_ready, m + 1)
                nc.vector.tensor_tensor(h[:, bass.ds(m, 1), :], h[:, bass.ds(m, 1), :], g_sig[b][:],
                                        ALU.add).then_inc(h_final, 1)

            def gate_pair(i, first=False):
                n = U_PLE + 6 * i
                split(n, 0, UK * P)
                if first:
                    down_tile(GROUPS - 1, KT - 2, 0, True)
                split(n + 1, 1, UK * P)
                if first:
                    down_tile(GROUPS - 1, KT - 1, 1, True)
                    norm_factor(2)
                    dve.wait_ge(ph_ready, 1)
                    nc.vector.tensor_tensor(p_lo[:], p_raw[:], p_hi[:].bitcast(F32), ALU.subtract).then_inc(pl_ready, 1)
                else:
                    ple_tile(2 * i - 1, 1)
                split(n + 2, 0, PK * P)
                split(n + 3, 1, UK * P)
                split(n + 4, 0, UK * P)
                ple_tile(2 * i, 0)
                split(n + 5, 1, PK * P)

            gate_pair(0, True)
            with dve.Fori(1, KT // 2) as i:
                gate_pair(i)
            ple_tile(KT - 1, 1)

            norm_factor(3)
            for m in range(KT):
                nc.vector.scalar_tensor_tensor(result[:, m, :], h[:, m, :], gain[:, 3, m:m + 1], rstd[:],
                                               ALU.mult, ALU.mult).then_inc(res_ready, 1)

        @block.tensor
        def _(pe):
            def blocks(out, slot, ks, hi, lo, k0, first, last, ready=None):
                for kk in range(ks):
                    if ready is not None:
                        pe.wait_ge(ready[0], ready[1] + k0 + kk + 1)
                    w1 = w_hi[slot][:, kk * P:(kk + 1) * P]
                    w2 = w_lo[slot][:, kk * P:(kk + 1) * P]
                    nc.tensor.matmul(out, w1, hi[:, k0 + kk, :], start=first and kk == 0, stop=False)
                    nc.tensor.matmul(out, w1, lo[:, k0 + kk, :], start=False, stop=False)
                    mm = nc.tensor.matmul(out, w2, hi[:, k0 + kk, :], start=False, stop=last and kk == ks - 1)
                mm.then_inc(unit_done, 1)

            def norm_sum(r):
                pe.wait_ge(sq_added, (KT + 1) * (r + 1))
                nc.tensor.matmul(px[:], ones[:], sq_sum[:], start=True, stop=True).then_inc(ms_done, 1)

            def mix(g, s):
                if s == 0:
                    pe.wait_ge(evac_done, NJ * g + NJ)
                    for c in range(CT):
                        nc.tensor.transpose(px[:, c * P:(c + 1) * P], stage[2][:, c * P:(c + 1) * P], ident[:])
                    for c in range(CT):
                        mm = nc.tensor.transpose(py[:, c * P:(c + 1) * P], stage[6][:, c * P:(c + 1) * P], ident[:])
                    mm.then_inc(vt_done, 1)
                if s < CT:
                    if s:
                        pe.wait_ge(sc_read, CT * g + s)
                    nc.tensor.matmul(ps[:, 0:(s + 1) * P], stage[4][:, s * P:(s + 1) * P],
                                     stage[5][:, 0:(s + 1) * P], start=True, stop=True).then_inc(sc_done, 1)
                if s < LEVELS:
                    pe.wait_ge(hg_upd, 9 * g + s + 1)
                    for c in range(CT):
                        mm = nc.tensor.matmul(pl[s % 2][:, c * P:(c + 1) * P], k[:, c * P:(c + 1) * P],
                                              q[:, c * P:(c + 1) * P], start=True, stop=True)
                    mm.then_inc(lvl_done, 1)
                if 1 <= s <= CT:
                    t = s - 1
                    pe.wait_ge(sc_prob, CT * g + t + 1)
                    if t == 0:
                        pe.wait_ge(v_copied, 2 * g + 2)
                    else:
                        pe.wait_ge(pt_copied, CT * g + t)
                    for j in range(t + 1):
                        mm = nc.tensor.transpose(py[:, j * P:(j + 1) * P], prob[t % 2][:, j * P:(j + 1) * P], ident[:])
                    mm.then_inc(pt_done, 1)
                if s == 5:
                    pe.wait_ge(pt_copied, CT * g + CT)
                    for j in range(CT):
                        mm = nc.tensor.matmul(py[:, j * P:S], v_att[:, j, :], prob_t[:, j, j * P:S],
                                              start=(j == 0), stop=(j == CT - 1))
                    mm.then_inc(att_out, 1)
                if s == 8:
                    pe.wait_ge(hg_upd, 9 * g + 9)
                    for c in range(CT):
                        mm = nc.tensor.transpose(px[:, c * P:(c + 1) * P], k[:, c * P:(c + 1) * P], ident[:])
                    mm.then_inc(kt_done, 1)
                if s == 9:
                    pe.wait_ge(kt_copied, g + 1)
                    for c in range(CT - 1):
                        mm = nc.tensor.matmul(px[:, c * P:(c + 1) * P], k_tok[:, c, :], v_hg[:, c, :],
                                              start=True, stop=True)
                    mm.then_inc(kv_done, 1)
                if s == 10:
                    pe.wait_ge(st_step, 3 * g + 3)
                    pe.wait_ge(lvl_masked, LEVELS * g + LEVELS + 1)
                    pe.wait_ge(y_att, g + 1)
                    for c in range(CT):
                        out = py[:, c * P:(c + 1) * P]
                        mm = nc.tensor.matmul(out, v_hg[:, c, :], intra[:, c, :], start=True, stop=(c == 0))
                        if c:
                            mm = nc.tensor.matmul(out, state[:, c - 1, :], q[:, c * P:(c + 1) * P],
                                                  start=False, stop=True)
                    mm.then_inc(hg_out, 1)
                if s == 11:
                    pe.wait_ge(hg_sq, g + 1)
                    nc.tensor.matmul(px[:], ones[:], o_sq[:], start=True, stop=True).then_inc(hg_ms, 1)

            def pair(hh, proj, mixing):
                for s in range(SU):
                    if proj:
                        j = s // 2
                        pe.wait_ge(lo_ready, SU * hh + s + 1)
                        if s % 2 == 0:
                            first = isinstance(hh, int)
                            if j == 6:
                                wait(pe, evac_done, NJ * hh)
                            elif j < 2:
                                if not first:
                                    pe.wait_ge(evac_done, NJ * hh - 2 + j)
                            else:
                                pe.wait_ge(evac_done, NJ * hh + j - 1)
                        blocks(pt[2 if j == 6 else j % 2][:], s % 2, UK, a_hi, a_lo, (s % 2) * UK,
                               s % 2 == 0, s % 2 == 1, (nl_ready, 0) if (not mixing and s < 2) else None)
                    if mixing:
                        mix(hh - 1, s)
                    elif s == 1:
                        norm_sum(0)

            pair(0, True, False)
            with pe.Fori(1, HEADS) as hh:
                pair(hh, True, True)
            pair(HEADS, False, True)

            def out_pair(i, first):
                for b in range(2):
                    m = 2 * i + b
                    if not (first and b == 0):
                        if not first:
                            pe.wait_ge(h_final, m - 1)
                    for u in range(2):
                        pe.wait_ge(lo_ready, U_OUT + 2 * m + u + 1)
                        blocks(pt[b][:], u, UK, y_hi, y_lo, u * UK, u == 0, u == 1,
                               (yl_ready, 0) if first and b == 0 else None)

            out_pair(0, True)
            with pe.Fori(1, KT // 2) as i:
                out_pair(i, False)

            def up_pair(g, i, first=False, waits=None):
                n = U_FFN + U_GRP * g + 4 * i
                for b in range(2):
                    if waits:
                        waits(b)
                    elif b == 0:
                        pe.wait_ge(cg_step, 4 * (FG * g + i - 1) + 1)
                    else:
                        pe.wait_ge(cv_step, 5 * (FG * g + i - 1) + 1)
                    for u in range(2):
                        pe.wait_ge(lo_ready, n + 2 * b + u + 1)
                        blocks(pt[b][:], u, UK, n_hi, n_lo, u * UK, u == 0, u == 1,
                               (nl_ready, KT) if first and b == 0 else None)
                    if first and b == 0:
                        norm_sum(1)

            def down(g, last):
                n = U_FFN + U_GRP * g + 4 * FG
                for m in range(2):
                    pe.wait_ge(lo_ready, n + m + 1)
                    pe.wait_ge(*((cg_step, 4 * (FG * g + FG - 1) + 1) if m == 0 else (cv_step, 5 * (FG * g + FG - 1) + 1)))
                    blocks(pt[m][:], m, FG, f_hi, f_lo, 0, True, True,
                           (fl_ready, FG * g) if m == 0 else None)
                with pe.Fori(1, KT // 2) as i:
                    for b in range(2):
                        m = 2 * i + b
                        pe.wait_ge(lo_ready, n + m + 1)
                        if last:
                            pe.wait_ge(h_final, KT + m - 1)
                        else:
                            pe.wait_ge(down_read, KT * g + m - 1)
                        blocks(pt[b][:], b, FG, f_hi, f_lo, 0, True, True)

            up_pair(0, 0, True, lambda b: pe.wait_ge(h_final, KT - 1 + b))
            with pe.Fori(1, FG) as i:
                up_pair(0, i)
            down(0, False)
            with pe.Fori(1, GROUPS - 1) as g:
                up_pair(g, 0, False, lambda b: pe.wait_ge(down_read, KT * g - 1 + b))
                with pe.Fori(1, FG) as i:
                    up_pair(g, i)
                down(g, False)
            up_pair(GROUPS - 1, 0, False, lambda b: pe.wait_ge(down_read, KT * (GROUPS - 1) - 1 + b))
            with pe.Fori(1, FG) as i:
                up_pair(GROUPS - 1, i)
            down(GROUPS - 1, True)

            def gate_pair(i, first=False):
                for b in range(2):
                    m = 2 * i + b
                    slots = [(3 * b + u) % 2 for u in range(3)]
                    n = U_PLE + 3 * m
                    if first:
                        pe.wait_ge(h_final, 2 * KT - 1 + b)
                    else:
                        pe.wait_ge(h_final, 2 * KT + m - 1)
                    for u in range(2):
                        pe.wait_ge(lo_ready, n + u + 1)
                        blocks(pt[b][:], slots[u], UK, n_hi, n_lo, u * UK, u == 0, u == 1,
                               (nl_ready, 2 * KT) if first and b == 0 else None)
                    if first and b == 0:
                        norm_sum(2)
                        pe.wait_ge(pl_ready, 1)
                    pe.wait_ge(lo_ready, n + 3)
                    blocks(pl[b][:], slots[2], PK, p_hi, p_lo, 0, True, True)

            gate_pair(0, True)
            with pe.Fori(1, KT // 2) as i:
                gate_pair(i)
            norm_sum(3)


def kernel(x, p, norm_mix, w_in, lb_logits, hg_norm, rel_bias, w_out, norm_ffn,
           w_up, conv_w, conv_b, w_down, norm_ple, w_ple_gate, w_ple_proj, final_norm):
    import numpy as np
    import concourse.bacc as bacc
    from concourse.bass_utils import run_bass_kernel_spmd as run

    f32 = [np.asarray(a) for a in (x, p, norm_mix, w_in, lb_logits, hg_norm, rel_bias, w_out, norm_ffn,
                                   w_up, conv_w, conv_b, w_down, norm_ple, w_ple_gate, w_ple_proj, final_norm)]
    (x, p, norm_mix, w_in, lb_logits, hg_norm, rel_bias, w_out, norm_ffn,
     w_up, conv_w, conv_b, w_down, norm_ple, w_ple_gate, w_ple_proj, final_norm) = f32
    c = np.ascontiguousarray

    def units(w, kt):
        rows, cols = w.shape
        g = rows // (P * kt)
        return w.reshape(g, kt, P, cols // P, P).transpose(3, 0, 2, 1, 4).reshape(cols // P, g, P, kt * P)

    order = np.array([part * HEADS + hd for hd in range(HEADS) for part in (1, 0, 2, 3, 4, 5, 6)])
    win = units(w_in[0], UK)[order].reshape(U_OUT, P, UK * P)
    rows = w_out[0].reshape(2, HEADS, P, D).transpose(1, 0, 2, 3).reshape(D, D)
    wout = units(rows, UK).reshape(2 * KT, P, UK * P)
    up_order = np.array([part * FFT + t for t in range(FFT) for part in (0, 1)])
    wup = units(w_up[0], UK)[up_order].reshape(4 * FFT, P, UK * P)
    wdown = units(w_down[0], FG).transpose(1, 0, 2, 3).reshape(GROUPS * KT, P, FG * P)
    wgate = units(w_ple_gate[0], UK).reshape(2 * KT, P, UK * P)
    wproj = units(w_ple_proj[0], PK).reshape(KT, P, PK * P)
    cv = np.concatenate([conv_w[0], conv_b], axis=0).reshape(4, 2 * FFT, P)[:, up_order].transpose(2, 1, 0)
    gains = np.concatenate([norm_mix, norm_ffn, norm_ple, final_norm[None]], axis=0).reshape(4, KT, P).transpose(2, 0, 1)
    lbt = lb_logits.reshape(2, HEADS, P).transpose(2, 0, 1)
    rel = np.minimum(2 * P, P + P + np.arange(P)[:, None] - np.arange(2 * P)[None, :])
    brow = rel_bias[0].T[rel].transpose(0, 2, 1)
    s, t = np.arange(P)[:, None], np.arange(P)[None, :]
    lv = [s == t] + [(s // (2 * m) == t // (2 * m)) & (s // m % 2 == 0) & (t // m % 2 == 1)
                     for m in (1, 2, 4, 8, 16, 32, 64)]
    masks = np.stack(lv, axis=1).astype(np.float32)
    ins = {
        "in_x": x[0].reshape(S, KT, P).transpose(2, 1, 0), "in_gains": gains, "in_w_in": win,
        "in_lb": lbt, "in_hgn": hg_norm.reshape(P, 1), "in_bias": brow, "in_w_out": wout, "in_w_up": wup,
        "in_conv": cv, "in_w_down": wdown, "in_w_gate": wgate, "in_w_proj": wproj,
        "in_p": p[0, 0].reshape(S, PK, P).transpose(2, 1, 0), "in_masks": masks,
        "in_eye": np.eye(P, dtype=np.float32),
    }
    ins = {n: c(a) for n, a in ins.items()}
    nc = bacc.Bacc("TRN2", target_bir_lowering=False, num_devices=1)
    args = [nc.dram_tensor(n, a.shape, mybir.dt.from_np(a.dtype), kind="ExternalInput").ap() for n, a in ins.items()]
    out = nc.dram_tensor("out_t", (P, KT, S), F32, kind="ExternalOutput").ap()
    build(nc, *args, out)
    r = run(nc, [ins], core_ids=[0])
    return c(r.results[0]["out_t"].transpose(2, 1, 0).reshape(1, S, D))
```

```python
from contextlib import ExitStack

import concourse.bass as bass
from concourse import mybir

F32 = mybir.dt.float32
F32R = mybir.dt.float32r
U32 = mybir.dt.uint32
ALU = mybir.AluOpType
ACT = mybir.ActivationFunctionType
AX = mybir.AxisListType

P = 128
S = 512
D = 2048
KT = D // P
HEADS = 8
NJ = 7
UK = 8
FFT = 5632 // P
GROUPS = 4
FG = FFT // GROUPS
PK = 2
CT = S // P
LEVELS = 8
EPS = 1e-6
LOWEST = -3.3895314e38
SU = 2 * NJ
EK = 7
GK = 9

U_OUT = HEADS * SU
ET = 4
U_FIN = U_OUT + 2 * ET
U_REST = U_FIN + 2
U_FFN = U_REST + 2 * (KT - ET)
U_GRP = 4 * FG + KT
U_PLE = U_FFN + GROUPS * U_GRP
U_END = U_PLE + 2 * KT


def level_offset(m):
    return 1024 - 1024 // m


def build(nc, xT, gains, w_in, lb_logits, hg_gain, bias_rows, w_early, w_finish, w_out,
          w_up, conv, w_down, w_gate, pT, masks, eye, outT):
    with ExitStack() as ctx:
        def sb(name, shape, dt=F32):
            return ctx.enter_context(nc.sbuf_tensor(name, shape, dt))

        def sem(name):
            return ctx.enter_context(nc.semaphore(name))

        raw = [sb(f"raw{i}", [P, FG * P]) for i in range(2)]
        w_hi = [sb(f"w_hi{i}", [P, FG * P], F32R) for i in range(2)]
        w_lo = [sb(f"w_lo{i}", [P, FG * P], F32R) for i in range(2)]
        rstd = sb("rstd", [P, S])
        root = sb("root", [P, S])
        sq_sum = sb("sq_sum", [P, S])
        sq = [sb(f"sq{i}", [P, S]) for i in range(2)]
        gain = sb("gain", [P, 4, KT])
        conv_c = sb("conv_c", [P, 2 * FFT, 4])
        ones = sb("ones", [P, P])
        ident = sb("ident", [P, P])
        lbl = sb("lbl", [P, 2, HEADS])
        lb = sb("lb", [P, 6, HEADS])
        lb_now = sb("lb_now", [P, 2])
        hgn = sb("hgn", [P, 1])
        bias_now = sb("bias_now", [P, 1])
        eps = sb("eps", [P, 1])
        neg_max = sb("neg_max", [P, 2])
        row_sum = sb("row_sum", [P, 2])
        row_inv = sb("row_inv", [P, 2])

        base = (nc.sbuf_base + 63) // 64 * 64
        R1, R2, RH = base, base + 65536, base + 131072

        def at(name, off, shape, dt=F32):
            return nc.alloc_sbuf_tensor_at(name, shape, dt, offset=off)

        a_hi = at("a_hi", R1, [P, KT, S], F32R)
        a_lo = at("a_lo", R1 + 32768, [P, KT, S], F32R)
        y_hi = at("y_hi", R1, [P, KT, S], F32R)
        y_lo = at("y_lo", R1 + 32768, [P, KT, S], F32R)
        f_hi = at("f_hi", R1, [P, FG, S], F32R)
        f_lo = at("f_lo", R1 + 22528, [P, FG, S], F32R)
        o = R1 + 45056
        u_gate = at("u_gate", o, [P, 520]); o += 2080
        u_val = at("u_val", o, [P, 520]); o += 2080
        c_gate = at("c_gate", o, [P, S]); o += 2048
        c_val = at("c_val", o, [P, S]); o += 2048
        s_gate = at("s_gate", o, [P, S]); o += 2048
        f_act = at("f_act", o, [P, S]); o += 2048
        p_raw = at("p_raw", R1, [P, PK, S])
        p_hi = at("p_hi", R1 + 4096, [P, PK, S], F32R)
        p_lo = at("p_lo", R1 + 8192, [P, PK, S], F32R)
        g_pre = [at(f"g_pre{i}", R1 + 12288 + 2048 * i, [P, S]) for i in range(2)]
        g_sig = [at(f"g_sig{i}", R1 + 16384 + 2048 * i, [P, S]) for i in range(2)]
        y = at("y", R2, [P, KT, S])
        o = R2 + 32768
        stage = [at(f"stage{j}", o + 2048 * j, [P, S]) for j in range(NJ)]; o += 2048 * NJ
        v_hg = at("v_hg", o, [P, CT, P]); o += 2048
        v_att = at("v_att", o, [P, CT, P]); o += 2048
        prob_t = at("prob_t", o, [P, CT, S]); o += 8192
        intra = at("intra", o, [P, CT, P]); o += 2048
        mask = at("mask", o, [P, P + (LEVELS - 1) * P // 2]); o += 4096
        assert o <= RH
        n_hi = at("n_hi", R2, [P, KT, S], F32R)
        n_lo = at("n_lo", R2 + 32768, [P, KT, S], F32R)
        result = at("result", R2, [P, KT, S])
        h = at("h", RH, [P, KT, S])
        o = RH
        q = at("q", o, [P, S]); o += 2048
        k = at("k", o, [P, S]); o += 2048
        fg = at("fg", o, [P, 1024]); o += 4096
        gate = at("gate", o, [P, S]); o += 2048
        og = at("og", o, [P, S]); o += 2048
        o_sq = at("o_sq", o, [P, S]); o += 2048
        o_rs = at("o_rs", o, [P, S]); o += 2048
        k_tok = at("k_tok", o, [P, CT, P]); o += 2048
        state = at("state", o, [P, CT - 1, P]); o += 2048
        prob = [at(f"prob{i}", o + 2048 * i, [P, S]) for i in range(2)]; o += 4096
        bias = at("bias", o, [P, HEADS, 2 * P]); o += 8192
        assert o <= RH + 32768

        pt = [ctx.enter_context(nc.psum_tensor(f"pt{i}", [P, S], F32)) for i in range(3)]
        pl = [ctx.enter_context(nc.psum_tensor(f"pl{i}", [P, S], F32)) for i in range(2)]
        px = ctx.enter_context(nc.psum_tensor("px", [P, S], F32))
        py = ctx.enter_context(nc.psum_tensor("py", [P, S], F32))
        ps = ctx.enter_context(nc.psum_tensor("ps", [P, S], F32))

        raw_in = [sem(f"raw_in{i}") for i in range(2)]
        hi_ready = sem("hi_ready")
        lo_ready = sem("lo_ready")
        unit_done = sem("unit_done")
        evac_done = sem("evac_done")
        x_in = [sem(f"x_in{i}") for i in range(8)]
        gain_in = sem("gain_in")
        const_in = sem("const_in")
        bias_in = sem("bias_in")
        p_in = sem("p_in")
        consts = sem("consts")
        nh_ready = sem("nh_ready")
        nl_ready = sem("nl_ready")
        sq_ready = sem("sq_ready")
        sq_added = sem("sq_added")
        ms_done = sem("ms_done")
        root_ready = sem("root_ready")
        rstd_ready = sem("rstd_ready")
        h_final = sem("h_final")
        lb_step = sem("lb_step")
        lb_exp = sem("lb_exp")
        bias_cut = sem("bias_cut")
        hg_in = sem("hg_in")
        hg_gate = sem("hg_gate")
        lb_set = sem("lb_set")
        hg_upd = sem("hg_upd")
        lvl_done = sem("lvl_done")
        lvl_masked = sem("lvl_masked")
        vt_done = sem("vt_done")
        v_copied = sem("v_copied")
        kt_done = sem("kt_done")
        kt_copied = sem("kt_copied")
        kv_done = sem("kv_done")
        st_step = sem("st_step")
        hg_out = sem("hg_out")
        hg_sq = sem("hg_sq")
        hg_og = sem("hg_og")
        hg_ms = sem("hg_ms")
        hg_root = sem("hg_root")
        hg_rs = sem("hg_rs")
        y_hg = sem("y_hg")
        sc_done = sem("sc_done")
        sc_read = sem("sc_read")
        sc_max = sem("sc_max")
        sc_exp = sem("sc_exp")
        sc_inv = sem("sc_inv")
        sc_prob = sem("sc_prob")
        pt_done = sem("pt_done")
        pt_copied = sem("pt_copied")
        att_out = sem("att_out")
        y_att = sem("y_att")
        yh_ready = sem("yh_ready")
        yl_ready = sem("yl_ready")
        cg_step = sem("cg_step")
        cv_step = sem("cv_step")
        down_read = sem("down_read")
        silu_done = sem("silu_done")
        fh_ready = sem("fh_ready")
        fl_ready = sem("fl_ready")
        ph_ready = sem("ph_ready")
        pl_ready = sem("pl_ready")
        gp_ready = sem("gp_ready")
        gs_ready = sem("gs_ready")
        gm_ready = sem("gm_ready")
        res_ready = sem("res_ready")
        stored = sem("stored")

        def wait(eng, s, value):
            if not (isinstance(value, int) and value <= 0):
                eng.wait_ge(s, value)

        def bank(hh, j):
            if isinstance(hh, int) and hh == 0 and j in (2, 3):
                return pl[j - 2]
            return pt[2 if j == 6 else j % 2]

        def odd_blocks(ap, m):
            return ap.rearrange("p (b two m) -> p b two m", two=2, m=m)[:, :, 1, :]

        def wait_apart(eng, s, value):
            if isinstance(value, int):
                wait(eng, s, value)
            else:
                ready = eng.snap(value)
                eng.wait_ge(consts, 1)
                eng.wait_ge(s, ready)

        block = ctx.enter_context(nc.Block())

        @block.sync
        def _(sp):
            def load(slot, src, width, freed):
                wait(sp, lo_ready, freed)
                sp.dma_start(raw[slot][:, 0:width], src).then_inc(raw_in[slot], 16)

            def load_x(i):
                sp.dma_start(h[:, 2 * i:2 * i + 2, :], xT[:, 2 * i:2 * i + 2, :]).then_inc(x_in[i], 16)

            load(0, w_in[0], UK * P, 0)
            for i in range(8):
                load_x(i)
                if i == 3:
                    load(1, w_in[1], UK * P, 0)
            with sp.Fori(1, U_OUT // 2) as i:
                load(0, w_in[2 * i], UK * P, 2 * i - 1)
                load(1, w_in[2 * i + 1], UK * P, 2 * i)
            for e in range(2 * ET):
                load(e % 2, w_early[e], EK * P, U_OUT + e - 1)
            load(0, w_finish[:, 0:4 * P], 4 * P, U_FIN - 1)
            load(1, w_finish[:, 4 * P:8 * P], 4 * P, U_FIN)
            sp.wait_ge(y_hg, HEADS)
            sp.wait_ge(y_att, HEADS)
            load_x(0)
            load_x(1)
            load(0, w_out[0], UK * P, U_REST - 1)
            load(1, w_out[1], UK * P, U_REST)
            for i in range(2, 5):
                load_x(i)
            load(0, w_out[2], UK * P, U_REST + 1)
            for i in range(5, 8):
                load_x(i)
            load(1, w_out[3], UK * P, U_REST + 2)
            with sp.Fori(2, KT - ET) as i:
                load(0, w_out[2 * i], UK * P, U_REST + 2 * i - 1)
                load(1, w_out[2 * i + 1], UK * P, U_REST + 2 * i)
            with sp.Fori(0, GROUPS) as g:
                with sp.Fori(0, 2 * FG) as i:
                    load(0, w_up[g * (4 * FG) + 2 * i], UK * P, U_FFN + U_GRP * g + 2 * i - 1)
                    load(1, w_up[g * (4 * FG) + 2 * i + 1], UK * P, U_FFN + U_GRP * g + 2 * i)
                with sp.Fori(0, KT // 2) as i:
                    load(0, w_down[g * KT + 2 * i], FG * P, U_FFN + U_GRP * g + 4 * FG + 2 * i - 1)
                    load(1, w_down[g * KT + 2 * i + 1], FG * P, U_FFN + U_GRP * g + 4 * FG + 2 * i)

            load(0, w_gate[0], GK * P, U_PLE - 1)
            load(1, w_gate[1], GK * P, U_PLE)
            sp.wait_ge(unit_done, U_PLE)
            sp.dma_start(p_raw[:], pT).then_inc(p_in, 16)
            with sp.Fori(1, KT) as i:
                load(0, w_gate[2 * i], GK * P, U_PLE + 2 * i - 1)
                load(1, w_gate[2 * i + 1], GK * P, U_PLE + 2 * i)
            for a, b in [(0, 2), (2, 4), (4, 6), (6, 8), (8, 10), (10, 12), (12, 14), (14, 15), (15, 16)]:
                sp.wait_ge(res_ready, b)
                sp.dma_start(outT[:, a:b, :], result[:, a:b, :]).then_inc(stored, 16)
            sp.wait_ge(stored, 9 * 16)

        @block.gpsimd
        def _(pool):
            nc.gpsimd.memset(ones[:], 1.0)
            nc.gpsimd.memset(eps[:], EPS).then_inc(consts, 1)
            for r in range(4):
                wait(pool, ms_done, r)
                nc.gpsimd.memset(sq_sum[:], 0.0).then_inc(sq_added, 1)
                with pool.Fori(0, KT // 2 - (r == 3)) as i:
                    for b in range(2):
                        n = r * (KT + 1) + 2 * i + b
                        pool.wait_ge(sq_ready, r * KT + 2 * i + b + 1)
                        pool.wait_ge(sq_added, n + 1)
                        nc.gpsimd.tensor_tensor(sq_sum[:], sq_sum[:], sq[b][:], ALU.add).then_inc(sq_added, 1)
                if r == 3:
                    pool.wait_ge(sq_ready, 4 * KT - 1)
                    pool.wait_ge(sq_added, 3 * (KT + 1) + KT - 1)
                    nc.gpsimd.tensor_tensor(sq_sum[:], sq_sum[:], sq[0][:], ALU.add).then_inc(sq_added, 1)

        @block.scalar
        def _(act):
            def split(n, slot, width, count=None):
                act.wait_ge(raw_in[slot], 16 * count)
                wait(act, unit_done, n - 1)
                nc.scalar.activation(w_hi[slot][:, 0:width], raw[slot][:, 0:width], ACT.Copy).then_inc(hi_ready, 1)

            def norm_high(m, dst, g):
                nc.scalar.activation(dst[:, bass.ds(m, 1), :], h[:, bass.ds(m, 1), :], ACT.Copy,
                                     scale=gain[:, g, bass.ds(m, 1)]).then_inc(nh_ready, 1)

            def square(m, b):
                nc.scalar.activation(sq[b][:], h[:, bass.ds(m, 1), :], ACT.Square).then_inc(sq_ready, 1)

            def norm_root(r):
                act.wait_ge(ms_done, r + 1)
                nc.scalar.activation(root[:], px[:], ACT.Sqrt, bias=eps[:], scale=1.0 / D).then_inc(root_ready, 1)

            act.dma_start(gain[:], gains).then_inc(gain_in, 16)
            act.wait_ge(gain_in, 16)
            act.wait_ge(consts, 1)
            split(0, 0, UK * P, 1)
            for m in range(KT):
                if m % 2 == 0:
                    act.wait_ge(x_in[m // 2], 16)
                norm_high(m, a_hi, 0)
                if m == 8:
                    split(1, 1, UK * P, 1)
            act.dma_start(ident[:], eye).then_inc(const_in, 16)
            act.dma_start(lbl[:], lb_logits).then_inc(const_in, 16)
            act.dma_start(hgn[:], hg_gain).then_inc(const_in, 16)
            act.dma_start(mask[:], masks).then_inc(const_in, 16)
            act.dma_start(conv_c[:], conv).then_inc(const_in, 16)
            for m in range(KT):
                wait(act, sq_added, m if m > 1 else 0)
                square(m, m % 2)
                if m in (0, 1, 5, 9, 13):
                    n = 2 + (0, 1, 5, 9, 13).index(m)
                    split(n, n % 2, UK * P, n // 2 + 1)
            act.wait_ge(nl_ready, KT)
            act.wait_ge(sq_ready, KT)
            act.wait_ge(lb_step, 1)
            nc.scalar.activation(lb[:, 1:3, :], lb[:, 1:3, :], ACT.Exp).then_inc(lb_exp, 1)
            act.dma_start(bias[:], bias_rows).then_inc(bias_in, 16)

            def mix(g, s):
                if s == 0:
                    act.wait_ge(evac_done, NJ * g + NJ)
                    nc.scalar.activation(fg[:, 0:S], stage[0][:], ACT.Sigmoid)
                    nc.scalar.activation(k[:], stage[0][:], ACT.Sigmoid, scale=-1.0)
                    nc.scalar.activation(q[:], stage[1][:], ACT.Silu).then_inc(hg_in, 1)
                    nc.scalar.activation(gate[:], stage[3][:], ACT.Silu).then_inc(hg_gate, 1)
                if s == 1:
                    act.wait_ge(vt_done, g + 1)
                    nc.scalar.activation(v_hg[:].rearrange("p c d -> p (c d)"), px[:], ACT.Copy).then_inc(v_copied, 1)
                    nc.scalar.activation(v_att[:].rearrange("p c d -> p (c d)"), py[:], ACT.Copy).then_inc(v_copied, 1)
                if 2 <= s <= 5:
                    t = s - 2
                    act.wait_ge(pt_done, CT * g + t + 1)
                    nc.scalar.activation(prob_t[:, 0:t + 1, t * P:(t + 1) * P],
                                         py[:, 0:(t + 1) * P].rearrange("p (j t) -> p j t", t=P),
                                         ACT.Copy).then_inc(pt_copied, 1)
                if 1 <= s <= 4:
                    t = s - 1
                    act.wait_ge(sc_max, CT * g + t + 1)
                    nc.scalar.activation(prob[t % 2][:, 0:(t + 1) * P], prob[t % 2][:, 0:(t + 1) * P], ACT.Exp,
                                         bias=neg_max[:, t % 2:t % 2 + 1],
                                         accum_out=row_sum[:, t % 2:t % 2 + 1]).then_inc(sc_exp, 1)
                if s == 6:
                    act.wait_ge(att_out, g + 1)
                    nc.scalar.activation(y[:, bass.ds(2 * g + 1, 1), :], py[:], ACT.Copy).then_inc(y_att, 1)
                if s == 9:
                    act.wait_ge(kt_done, g + 1)
                    nc.scalar.activation(k_tok[:].rearrange("p c d -> p (c d)"), px[:], ACT.Copy).then_inc(kt_copied, 1)
                if s == 11:
                    act.wait_ge(hg_og, g + 1)
                    nc.scalar.activation(o_sq[:], py[:], ACT.Square).then_inc(hg_sq, 1)
                if s == 12:
                    act.wait_ge(hg_ms, g + 1)
                    nc.scalar.activation(o_rs[:], px[:], ACT.Sqrt, bias=eps[:], scale=1.0 / P).then_inc(hg_root, 1)

            def y_split(kk):
                nc.scalar.activation(y_hi[:, kk, :], y[:, kk, :], ACT.Copy).then_inc(yh_ready, 1)

            def pair(hh, mixing):
                for s in range(SU):
                    if mixing or s >= 7:
                        split(SU * hh + s, s % 2, UK * P, NJ * hh + s // 2 + 1)
                    if s >= 1 and mixing:
                        mix(hh - 1, s - 1)
                    if not mixing and s == 7:
                        norm_root(0)

            pair(0, False)
            with act.Fori(1, HEADS) as hh:
                pair(hh, True)
            split(U_OUT, 0, EK * P, U_OUT // 2 + 1)
            for s in range(13):
                if s in (3, 5, 7, 9, 11):
                    e = (s + 1) // 2
                    split(U_OUT + e, e % 2, EK * P, (U_OUT + e) // 2 + 1)
                if s == 12:
                    split(U_OUT + 7, 1, EK * P, U_OUT // 2 + 4)
                mix(HEADS - 1, s)
                if s == 0:
                    split(U_OUT + 1, 1, EK * P, U_OUT // 2 + 1)
                for kk in range(4 * s, min(4 * s + 4, KT - 2)):
                    y_split(kk)
            act.wait_ge(y_hg, HEADS)
            y_split(KT - 2)
            y_split(KT - 1)
            split(U_FIN, 0, 4 * P, U_FIN // 2 + 1)
            split(U_FIN + 1, 1, 4 * P, U_FIN // 2 + 1)

            def after_h(r, m, b, g, dst):
                wait_apart(act, h_final, (r - 1) * KT + m + 1)
                wait(act, sq_added, r * (KT + 1) + m)
                if dst is not None:
                    norm_high(m, dst, g)
                square(m, b)

            def out_splits(m):
                n = U_REST + 2 * (m - ET)
                split(n, 0, UK * P, U_REST // 2 + m - ET + 1)
                split(n + 1, 1, UK * P, U_REST // 2 + m - ET + 1)

            out_splits(ET)
            act.wait_ge(yl_ready, KT)
            for m in range(ET):
                after_h(1, m, m % 2, 1, n_hi)
            out_splits(ET + 1)
            after_h(1, ET, 0, 1, n_hi)
            with act.Fori(ET // 2 + 1, KT // 2) as i:
                for b in range(2):
                    out_splits(2 * i + b)
                    after_h(1, 2 * i + b - 1, (b + 1) % 2, 1, n_hi)

            def up_pair(g, i, head=None, root=False):
                n = U_FFN + U_GRP * g + 4 * i
                c = U_FFN // 2 + U_GRP // 2 * g + 2 * i
                split(n, 0, UK * P, c + 1)
                split(n + 1, 1, UK * P, c + 1)
                if head:
                    head()
                else:
                    finish_value(g, i - 1)
                split(n + 2, 0, UK * P, c + 2)
                split(n + 3, 1, UK * P, c + 2)
                if root:
                    norm_root(1)
                act.wait_ge(cg_step, 4 * (FG * g + i) + 4)
                nc.scalar.activation(s_gate[:], c_gate[:], ACT.Silu).then_inc(silu_done, 1)

            def finish_value(g, i):
                wait_apart(act, cv_step, 5 * (FG * g + i) + 5)
                nc.scalar.activation(f_hi[:, bass.ds(i, 1), :], f_act[:], ACT.Copy).then_inc(fh_ready, 1)

            def down(g, last):
                n = U_FFN + U_GRP * g + 4 * FG
                c = (U_FFN + 4 * FG) // 2 + U_GRP // 2 * g
                split(n, 0, FG * P, c + 1)
                finish_value(g, FG - 1)
                split(n + 1, 1, FG * P, c + 1)

                def two(i):
                    for b in range(2):
                        split(n + 2 * i + b, b, FG * P, c + i + 1)
                        if last:
                            after_h(2, 2 * i + b - 2, b, 2, n_hi)
                with act.Fori(1, KT // 2) as i:
                    two(i)

            up_pair(0, 0, lambda: after_h(1, KT - 1, 1, 1, n_hi), True)
            with act.Fori(1, FG) as i:
                up_pair(0, i)
            down(0, False)
            with act.Fori(1, GROUPS - 1) as g:
                up_pair(g, 0, lambda: None)
                with act.Fori(1, FG) as i:
                    up_pair(g, i)
                down(g, False)
            up_pair(GROUPS - 1, 0, lambda: None)
            with act.Fori(1, FG) as i:
                up_pair(GROUPS - 1, i)
            down(GROUPS - 1, True)

            def sigmoid(m, b):
                act.wait_ge(gp_ready, m + 1)
                nc.scalar.activation(g_sig[b][:], g_pre[b][:], ACT.Sigmoid).then_inc(gs_ready, 1)
                after_h(3, m, b, 3, None)

            def gate_splits(m):
                split(U_PLE + 2 * m, 0, GK * P, U_PLE // 2 + m + 1)
                split(U_PLE + 2 * m + 1, 1, GK * P, U_PLE // 2 + m + 1)

            split(U_PLE, 0, GK * P, U_PLE // 2 + 1)
            after_h(2, KT - 2, 0, 2, n_hi)
            split(U_PLE + 1, 1, GK * P, U_PLE // 2 + 1)
            after_h(2, KT - 1, 1, 2, n_hi)
            act.wait_ge(p_in, 16)
            nc.scalar.activation(p_hi[:], p_raw[:], ACT.Copy).then_inc(ph_ready, 1)
            gate_splits(1)
            norm_root(2)
            sigmoid(0, 0)
            with act.Fori(1, KT // 2) as i:
                for b in range(2):
                    gate_splits(2 * i + b)
                    sigmoid(2 * i + b - 1, (b + 1) % 2)
            sigmoid(KT - 1, 1)
            norm_root(3)

        @block.vector
        def _(dve):
            def split(n, slot, width):
                dve.wait_ge(hi_ready, n + 1)
                nc.vector.tensor_tensor(w_lo[slot][:, 0:width], raw[slot][:, 0:width],
                                        w_hi[slot][:, 0:width].bitcast(F32), ALU.subtract).then_inc(lo_ready, 1)

            def norm_low(c, m, dst, hi, g):
                dve.wait_ge(nh_ready, c + 1)
                nc.vector.scalar_tensor_tensor(dst[:, bass.ds(m, 1), :], h[:, bass.ds(m, 1), :],
                                               gain[:, g, bass.ds(m, 1)],
                                               hi[:, bass.ds(m, 1), :].bitcast(F32),
                                               ALU.mult, ALU.subtract).then_inc(nl_ready, 1)

            def norm_factor(r):
                dve.wait_ge(root_ready, r + 1)
                nc.vector.reciprocal(rstd[:], root[:]).then_inc(rstd_ready, 1)
                dve.wait_ge(rstd_ready, r + 1)

            nc.vector.memset(intra[:], 0.0).then_inc(lvl_masked, 1)
            split(0, 0, UK * P)
            for m in range(KT):
                norm_low(m, m, a_lo, a_hi, 0)
                if m == 8:
                    split(1, 1, UK * P)

            def head_constants():
                dve.wait_ge(const_in, 5 * 16)
                nc.vector.tensor_tensor(lb[:, 0, :], lbl[:, 0, :], lbl[:, 1, :], ALU.max).then_inc(lb_set, 1)
                dve.wait_ge(lb_set, 1)
                nc.vector.tensor_tensor(lb[:, 1, :], lbl[:, 0, :], lb[:, 0, :], ALU.subtract)
                nc.vector.tensor_tensor(lb[:, 2, :], lbl[:, 1, :], lb[:, 0, :], ALU.subtract).then_inc(lb_step, 1)
                dve.wait_ge(lb_exp, 1)
                nc.vector.tensor_tensor(lb[:, 3, :], lb[:, 1, :], lb[:, 2, :], ALU.add).then_inc(lb_step, 1)
                dve.wait_ge(lb_step, 2)
                nc.vector.reciprocal(lb[:, 3, :], lb[:, 3, :]).then_inc(lb_step, 1)
                dve.wait_ge(lb_step, 3)
                nc.vector.tensor_tensor(lb[:, 4, :], lb[:, 1, :], lb[:, 3, :], ALU.mult).then_inc(lb_step, 1)
                dve.wait_ge(lb_step, 4)
                nc.vector.tensor_scalar(lb[:, 5, :], lb[:, 4, :], -1.0, 1.0, ALU.mult, ALU.add).then_inc(lb_step, 1)
                dve.wait_ge(lb_step, 5)
                dve.wait_ge(bias_in, 16)
                nc.vector.memset(bias[0:64, :, P + 64:2 * P], LOWEST).then_inc(bias_cut, 1)

            def evac(hh, j):
                dve.wait_ge(unit_done, SU * hh + 2 * j + 2)
                if j in (0, 1):
                    wait(dve, hg_in, hh)
                elif j == 3:
                    wait(dve, hg_gate, hh)
                elif j == 2:
                    wait(dve, vt_done, hh)
                elif j < 6:
                    wait(dve, sc_done, CT * hh)
                nc.vector.tensor_tensor(stage[j][:], bank(hh, j)[:], rstd[:],
                                        ALU.mult).then_inc(evac_done, 1)

            def softmax_head(g, t):
                dve.wait_ge(sc_done, CT * g + t + 1)
                if t >= 2:
                    dve.wait_ge(pt_done, CT * g + t - 1)
                dst = prob[t % 2]
                scale = float(P) ** -0.5
                if t >= 2:
                    nc.vector.tensor_scalar(dst[:, 0:(t - 1) * P], ps[:, 0:(t - 1) * P], scale,
                                            bias_now[:, 0:1], ALU.mult, ALU.add)
                lo = max(t - 1, 0) * P
                nc.vector.scalar_tensor_tensor(dst[:, lo:(t + 1) * P], ps[:, lo:(t + 1) * P], scale,
                                               bias[:, bass.ds(g, 1), (P if t == 0 else 0):2 * P],
                                               ALU.mult, ALU.add).then_inc(sc_read, 1)
                dve.wait_ge(sc_read, CT * g + t + 1)
                nc.vector.tensor_reduce(neg_max[:, t % 2:t % 2 + 1], dst[:, 0:(t + 1) * P], AX.X, ALU.max,
                                        negate=True).then_inc(sc_max, 1)

            def softmax_tail(g, t):
                dve.wait_ge(sc_exp, CT * g + t + 1)
                nc.vector.reciprocal(row_inv[:, t % 2:t % 2 + 1], row_sum[:, t % 2:t % 2 + 1]).then_inc(sc_inv, 1)
                dve.wait_ge(sc_inv, CT * g + t + 1)
                nc.vector.tensor_scalar(prob[t % 2][:, 0:(t + 1) * P], prob[t % 2][:, 0:(t + 1) * P],
                                        row_inv[:, t % 2:t % 2 + 1], None, ALU.mult).then_inc(sc_prob, 1)

            def halves(buf, off, m):
                return buf[:, off:off + S].rearrange("p (b two m) -> p b two m", two=2, m=m)

            def mix(g, s):
                if 1 <= s <= 4:
                    softmax_head(g, s - 1)
                if s == 0:
                    nc.vector.tensor_copy(lb_now[:], lb[:, 4:6, bass.ds(g, 1)].rearrange("p a b -> p (a b)"))
                    nc.vector.tensor_copy(bias_now[:], bias[:, bass.ds(g, 1), 0:1].rearrange("p a b -> p (a b)")).then_inc(lb_set, 1)
                    dve.wait_ge(hg_in, g + 1)
                    dve.wait_ge(lb_set, g + 2)
                    nc.vector.tensor_scalar(k[:], k[:], lb_now[:, 1:2], None, ALU.mult)
                    nc.vector.tensor_scalar(fg[:, 0:S], fg[:, 0:S], lb_now[:, 1:2], lb_now[:, 0:1],
                                            ALU.mult, ALU.add).then_inc(hg_upd, 1)
                if 1 <= s <= LEVELS:
                    lvl = s - 1
                    dve.wait_ge(lvl_done, LEVELS * g + lvl + 1)
                    dve.wait_ge(hg_upd, 9 * g + s)
                    dve.wait_ge(lvl_masked, LEVELS * g + s)
                    if s == 1:
                        nc.vector.tensor_tensor(q[:], q[:], fg[:, 0:S], ALU.mult).then_inc(hg_upd, 1)
                    else:
                        m = 2 ** (s - 2)
                        nb = S // m
                        f_m = fg[:, level_offset(m):level_offset(m) + nb].rearrange("p (b two) -> p b two", two=2)
                        qv, kv = halves(q, 0, m), halves(k, 0, m)
                        nc.vector.tensor_tensor(qv[:, :, 1, :], qv[:, :, 1, :],
                                                f_m[:, :, 0:1].to_broadcast([P, nb // 2, m]), ALU.mult)
                        nc.vector.tensor_tensor(kv[:, :, 0, :], kv[:, :, 0, :],
                                                f_m[:, :, 1:2].to_broadcast([P, nb // 2, m]), ALU.mult)
                        nxt = level_offset(2 * m)
                        nc.vector.tensor_tensor(fg[:, nxt:nxt + nb // 2], f_m[:, :, 0], f_m[:, :, 1],
                                                ALU.mult).then_inc(hg_upd, 1)
                    if lvl == 0:
                        nc.vector.copy_predicated(
                            intra[:], mask[:, None, 0:P].bitcast(U32).to_broadcast([P, CT, P]),
                            pl[0][:].rearrange("p (c t) -> p c t", t=P)).then_inc(lvl_masked, 1)
                    else:
                        m = 2 ** (lvl - 1)
                        off = P + (lvl - 1) * P // 2
                        nc.vector.copy_predicated(
                            intra[:].rearrange("p c (b two m) -> p c b two m", two=2, m=m)[:, :, :, 1, :],
                            mask[:, off:off + P // 2].bitcast(U32).rearrange("p (o b m) -> p o b m", o=1, m=m)
                            .to_broadcast([P, CT, P // (2 * m), m]),
                            pl[lvl % 2][:, 0:S // 2].rearrange("p (c b m) -> p c b m", c=CT, m=m)
                        ).then_inc(lvl_masked, 1)
                if s == 10:
                    dve.wait_ge(kv_done, g + 1)
                    t128 = level_offset(P)
                    nc.vector.tensor_copy(state[:, 0, :], px[:, 0:P]).then_inc(st_step, 1)
                    for c in (1, 2):
                        dve.wait_ge(st_step, 3 * g + c)
                        nc.vector.scalar_tensor_tensor(state[:, c, :], state[:, c - 1, :], fg[:, t128 + c:t128 + c + 1],
                                                       px[:, c * P:(c + 1) * P], ALU.mult, ALU.add).then_inc(st_step, 1)
                if s == 11:
                    dve.wait_ge(hg_out, g + 1)
                    dve.wait_ge(hg_gate, g + 1)
                    nc.vector.scalar_tensor_tensor(og[:], py[:], hgn[:, 0:1], gate[:], ALU.mult, ALU.mult).then_inc(hg_og, 1)
                if s == 12:
                    dve.wait_ge(hg_root, g + 1)
                    nc.vector.reciprocal(o_rs[:], o_rs[:]).then_inc(hg_rs, 1)
                    dve.wait_ge(hg_rs, g + 1)
                    dve.wait_ge(hg_og, g + 1)
                    nc.vector.tensor_tensor(y[:, bass.ds(2 * g, 1), :], og[:], o_rs[:], ALU.mult).then_inc(y_hg, 1)
                if 1 <= s <= 4:
                    softmax_tail(g, s - 1)

            def y_split(kk):
                dve.wait_ge(yh_ready, kk + 1)
                nc.vector.tensor_tensor(y_lo[:, kk, :], y[:, kk, :], y_hi[:, kk, :].bitcast(F32),
                                        ALU.subtract).then_inc(yl_ready, 1)

            def pair(hh, mixing):
                for s in range(SU):
                    if mixing and s >= 3 and s % 2 == 1:
                        evac(hh, (s - 3) // 2)
                    if not mixing and s == 7:
                        head_constants()
                    if not mixing and s >= 2:
                        split(s, s % 2, UK * P)
                    if not mixing and s >= 7:
                        if s == 7:
                            norm_factor(0)
                        for j in {7: (0, 1), 8: (2,), 9: (3,), 11: (4,), 13: (5,)}.get(s, ()):
                            evac(hh, j)
                    if mixing and s == 1:
                        evac(hh - 1, NJ - 1)
                    if mixing:
                        split(SU * hh + s, s % 2, UK * P)
                    if s >= 1 and mixing:
                        mix(hh - 1, s - 1)

            pair(0, False)
            with dve.Fori(1, HEADS) as hh:
                pair(hh, True)
            split(U_OUT, 0, EK * P)
            evac(HEADS - 1, NJ - 1)
            for s in range(13):
                if s in (3, 5, 7, 9, 11):
                    e = (s + 1) // 2
                    split(U_OUT + e, e % 2, EK * P)
                if s == 12:
                    split(U_OUT + 7, 1, EK * P)
                mix(HEADS - 1, s)
                if s == 0:
                    split(U_OUT + 1, 1, EK * P)
                for kk in range(4 * s, min(4 * s + 4, KT - 2)):
                    y_split(kk)
            y_split(KT - 2)
            y_split(KT - 1)
            split(U_FIN, 0, 4 * P)
            split(U_FIN + 1, 1, 4 * P)

            def out_tile(m, bank, done):
                dve.wait_ge(unit_done, done)
                nc.vector.tensor_tensor(h[:, bass.ds(m, 1), :], h[:, bass.ds(m, 1), :], bank[:],
                                        ALU.add).then_inc(h_final, 1)
                norm_low(KT + m, m, n_lo, n_hi, 1)

            def out_splits(m):
                split(U_REST + 2 * (m - ET), 0, UK * P)
                split(U_REST + 2 * (m - ET) + 1, 1, UK * P)

            split(U_REST, 0, UK * P)
            dve.wait_ge(x_in[0], 32)
            out_tile(0, pt[0], U_FIN + 1)
            out_tile(1, pt[1], U_FIN + 1)
            split(U_REST + 1, 1, UK * P)
            dve.wait_ge(x_in[1], 32)
            out_tile(2, pt[2], U_REST)
            out_tile(3, pl[0], U_REST)
            for i in range(2, 8):
                dve.wait_ge(x_in[i], 32)
            out_splits(ET + 1)
            out_tile(ET, pt[0], U_REST + 2)
            with dve.Fori(ET // 2 + 1, KT // 2) as i:
                for b in range(2):
                    m = 2 * i + b
                    out_splits(m)
                    out_tile(m - 1, pt[(b + 1) % 2], U_REST + 2 * (m - ET))

            def conv_tile(u, c, steps, count, col, bank, done):
                dve.wait_ge(unit_done, done)
                nc.vector.tensor_tensor(u[:, 2:2 + S], pt[bank][:], rstd[:], ALU.mult).then_inc(steps, 1)
                dve.wait_ge(steps, count + 1)
                nc.vector.tensor_scalar(c[:], u[:, 2:2 + S], conv_c[:, bass.ds(col, 1), 2:3],
                                        conv_c[:, bass.ds(col, 1), 3:4], ALU.mult, ALU.add).then_inc(steps, 1)
                for tap in (1, 0):
                    dve.wait_ge(steps, count + 3 - tap)
                    nc.vector.scalar_tensor_tensor(c[:], u[:, tap:tap + S], conv_c[:, bass.ds(col, 1), tap:tap + 1],
                                                   c[:], ALU.mult, ALU.add).then_inc(steps, 1)

            def gate_tile(g, i):
                t = FG * g + i
                wait(dve, silu_done, t)
                conv_tile(u_gate, c_gate, cg_step, 4 * t, 2 * t, 0, U_FFN + U_GRP * g + 4 * i + 2)

            def value_tile(g, i):
                t = FG * g + i
                conv_tile(u_val, c_val, cv_step, 5 * t, 2 * t + 1, 1, U_FFN + U_GRP * g + 4 * i + 4)
                dve.wait_ge(cv_step, 5 * t + 4)
                dve.wait_ge(silu_done, t + 1)
                nc.vector.tensor_tensor(f_act[:], s_gate[:], c_val[:], ALU.mult).then_inc(cv_step, 1)
                dve.wait_ge(fh_ready, t + 1)
                nc.vector.tensor_tensor(f_lo[:, bass.ds(i, 1), :], f_act[:], f_hi[:, bass.ds(i, 1), :].bitcast(F32),
                                        ALU.subtract).then_inc(fl_ready, 1)

            def down_tile(g, m, b, last):
                dve.wait_ge(unit_done, U_FFN + U_GRP * g + 4 * FG + m + 1)
                nc.vector.tensor_tensor(h[:, bass.ds(m, 1), :], h[:, bass.ds(m, 1), :], pt[b][:],
                                        ALU.add).then_inc(h_final if last else down_read, 1)
                if last:
                    norm_low(2 * KT + m, m, n_lo, n_hi, 2)

            def up_pair(g, i, head=None, factor=False):
                n = U_FFN + U_GRP * g + 4 * i
                split(n, 0, UK * P)
                if head:
                    head(0)
                split(n + 1, 1, UK * P)
                if head:
                    head(1)
                else:
                    value_tile(g, i - 1)
                split(n + 2, 0, UK * P)
                split(n + 3, 1, UK * P)
                if factor:
                    norm_factor(1)
                gate_tile(g, i)

            def down(g, last):
                n = U_FFN + U_GRP * g + 4 * FG
                split(n, 0, FG * P)
                value_tile(g, FG - 1)
                split(n + 1, 1, FG * P)
                with dve.Fori(1, KT // 2) as i:
                    for b in range(2):
                        split(n + 2 * i + b, b, FG * P)
                        down_tile(g, 2 * i + b - 2, b, last)

            def first_ffn(b):
                if b:
                    out_tile(KT - 1, pt[1], U_FFN)
                    nc.vector.memset(u_gate[:, 0:2], 0.0)
                    nc.vector.memset(u_val[:, 0:2], 0.0)

            up_pair(0, 0, first_ffn, True)
            with dve.Fori(1, FG) as i:
                up_pair(0, i)
            down(0, False)
            with dve.Fori(1, GROUPS - 1) as g:
                up_pair(g, 0, lambda b: down_tile(g - 1, KT - 2 + b, b, False))
                with dve.Fori(1, FG) as i:
                    up_pair(g, i)
                down(g, False)
            up_pair(GROUPS - 1, 0, lambda b: down_tile(GROUPS - 2, KT - 2 + b, b, False))
            with dve.Fori(1, FG) as i:
                up_pair(GROUPS - 1, i)
            down(GROUPS - 1, True)

            def ple_tile(m, b):
                dve.wait_ge(unit_done, U_PLE + 2 * m + 2)
                nc.vector.tensor_tensor(g_pre[b][:], pt[b][:], rstd[:], ALU.mult).then_inc(gp_ready, 1)
                dve.wait_ge(gs_ready, m + 1)
                nc.vector.tensor_tensor(g_sig[b][:], g_sig[b][:], pl[b][:], ALU.mult).then_inc(gm_ready, 1)
                dve.wait_ge(gm_ready, m + 1)
                nc.vector.tensor_tensor(h[:, bass.ds(m, 1), :], h[:, bass.ds(m, 1), :], g_sig[b][:],
                                        ALU.add).then_inc(h_final, 1)

            def gate_splits(m):
                split(U_PLE + 2 * m, 0, GK * P)
                split(U_PLE + 2 * m + 1, 1, GK * P)

            split(U_PLE, 0, GK * P)
            down_tile(GROUPS - 1, KT - 2, 0, True)
            split(U_PLE + 1, 1, GK * P)
            down_tile(GROUPS - 1, KT - 1, 1, True)
            dve.wait_ge(ph_ready, 1)
            nc.vector.tensor_tensor(p_lo[:], p_raw[:], p_hi[:].bitcast(F32), ALU.subtract).then_inc(pl_ready, 1)
            gate_splits(1)
            norm_factor(2)
            ple_tile(0, 0)
            with dve.Fori(1, KT // 2) as i:
                for b in range(2):
                    gate_splits(2 * i + b)
                    ple_tile(2 * i + b - 1, (b + 1) % 2)
            ple_tile(KT - 1, 1)

            norm_factor(3)
            for m in range(KT):
                nc.vector.scalar_tensor_tensor(result[:, m, :], h[:, m, :], gain[:, 3, m:m + 1], rstd[:],
                                               ALU.mult, ALU.mult).then_inc(res_ready, 1)

        @block.tensor
        def _(pe):
            def blocks(out, slot, ks, hi, lo, k0, first, last, ready=None, at=0, done=True):
                for kk in range(ks):
                    if ready is not None:
                        pe.wait_ge(ready[0], ready[1] + k0 + kk + 1)
                    w1 = w_hi[slot][:, (at + kk) * P:(at + kk + 1) * P]
                    w2 = w_lo[slot][:, (at + kk) * P:(at + kk + 1) * P]
                    nc.tensor.matmul(out, w1, hi[:, k0 + kk, :], start=first and kk == 0, stop=False)
                    nc.tensor.matmul(out, w1, lo[:, k0 + kk, :], start=False, stop=False)
                    mm = nc.tensor.matmul(out, w2, hi[:, k0 + kk, :], start=False, stop=last and kk == ks - 1)
                if done:
                    mm.then_inc(unit_done, 1)

            def norm_sum(r):
                if r < 3:
                    pe.wait_ge(sq_added, (KT + 1) * (r + 1))
                    nc.tensor.matmul(px[:], ones[:], sq_sum[:], start=True, stop=True).then_inc(ms_done, 1)
                else:
                    pe.wait_ge(sq_added, (KT + 1) * (r + 1) - 1)
                    nc.tensor.matmul(px[:], ones[:], sq_sum[:], start=True, stop=False)
                    pe.wait_ge(sq_ready, 4 * KT)
                    nc.tensor.matmul(px[:], ones[:], sq[1][:], start=False, stop=True).then_inc(ms_done, 1)

            def mix(g, s):
                if s == 0:
                    pe.wait_ge(evac_done, NJ * g + NJ)
                    for c in range(CT):
                        nc.tensor.transpose(px[:, c * P:(c + 1) * P], stage[2][:, c * P:(c + 1) * P], ident[:])
                    for c in range(CT):
                        mm = nc.tensor.transpose(py[:, c * P:(c + 1) * P], stage[6][:, c * P:(c + 1) * P], ident[:])
                    mm.then_inc(vt_done, 1)
                if s < CT:
                    if s:
                        pe.wait_ge(sc_read, CT * g + s)
                    nc.tensor.matmul(ps[:, 0:(s + 1) * P], stage[4][:, s * P:(s + 1) * P],
                                     stage[5][:, 0:(s + 1) * P], start=True, stop=True).then_inc(sc_done, 1)
                if s < LEVELS:
                    pe.wait_ge(hg_upd, 9 * g + s + 1)
                    for c in range(CT):
                        m = 2 ** (s - 1) if s else 0
                        qc = q[:, c * P:(c + 1) * P]
                        out = pl[s % 2][:, c * P:(c + 1) * P] if s == 0 else pl[s % 2][:, c * P // 2:(c + 1) * P // 2]
                        mm = nc.tensor.matmul(out if s == 0 else out.rearrange("p (b m) -> p b m", m=m),
                                              k[:, c * P:(c + 1) * P], qc if s == 0 else odd_blocks(qc, m),
                                              start=True, stop=True)
                    mm.then_inc(lvl_done, 1)
                if 1 <= s <= CT:
                    t = s - 1
                    pe.wait_ge(sc_prob, CT * g + t + 1)
                    if t == 0:
                        pe.wait_ge(v_copied, 2 * g + 2)
                    else:
                        pe.wait_ge(pt_copied, CT * g + t)
                    for j in range(t + 1):
                        mm = nc.tensor.transpose(py[:, j * P:(j + 1) * P], prob[t % 2][:, j * P:(j + 1) * P], ident[:])
                    mm.then_inc(pt_done, 1)
                if s == 5:
                    pe.wait_ge(pt_copied, CT * g + CT)
                    for j in range(CT):
                        mm = nc.tensor.matmul(py[:, j * P:S], v_att[:, j, :], prob_t[:, j, j * P:S],
                                              start=(j == 0), stop=(j == CT - 1))
                    mm.then_inc(att_out, 1)
                if s == 8:
                    pe.wait_ge(hg_upd, 9 * g + 9)
                    for c in range(CT):
                        mm = nc.tensor.transpose(px[:, c * P:(c + 1) * P], k[:, c * P:(c + 1) * P], ident[:])
                    mm.then_inc(kt_done, 1)
                if s == 9:
                    pe.wait_ge(kt_copied, g + 1)
                    for c in range(CT - 1):
                        mm = nc.tensor.matmul(px[:, c * P:(c + 1) * P], k_tok[:, c, :], v_hg[:, c, :],
                                              start=True, stop=True)
                    mm.then_inc(kv_done, 1)
                if s == 10:
                    pe.wait_ge(st_step, 3 * g + 3)
                    pe.wait_ge(lvl_masked, LEVELS * g + LEVELS + 1)
                    pe.wait_ge(y_att, g + 1)
                    for c in range(CT):
                        out = py[:, c * P:(c + 1) * P]
                        mm = nc.tensor.matmul(out, v_hg[:, c, :], intra[:, c, :], start=True, stop=(c == 0))
                        if c:
                            mm = nc.tensor.matmul(out, state[:, c - 1, :], q[:, c * P:(c + 1) * P],
                                                  start=False, stop=True)
                    mm.then_inc(hg_out, 1)
                if s == 11:
                    pe.wait_ge(hg_sq, g + 1)
                    nc.tensor.matmul(px[:], ones[:], o_sq[:], start=True, stop=True).then_inc(hg_ms, 1)

            def pair(hh, mixing):
                for s in range(SU):
                    j = s // 2
                    pe.wait_ge(lo_ready, SU * hh + s + 1)
                    if s % 2 == 0:
                        if not mixing:
                            wait(pe, evac_done, j - 3 if j in (4, 5) else 0)
                        elif j == 6:
                            pe.wait_ge(evac_done, NJ * hh)
                        elif j < 2:
                            pe.wait_ge(evac_done, NJ * hh - 2 + j)
                        else:
                            pe.wait_ge(evac_done, NJ * hh + j - 1)
                    blocks(bank(hh, j)[:], s % 2, UK, a_hi, a_lo, (s % 2) * UK,
                           s % 2 == 0, s % 2 == 1, (nl_ready, 0) if (not mixing and s < 2) else None)
                    if mixing:
                        mix(hh - 1, s)
                    elif s == 5:
                        norm_sum(0)

            pair(0, False)
            with pe.Fori(1, HEADS) as hh:
                pair(hh, True)
            early = [pt[0], pt[1], pt[2], pl[0]]

            def early_blocks(e, at, ks):
                if at == 0:
                    pe.wait_ge(lo_ready, U_OUT + e + 1)
                blocks(early[e // 2][:], e % 2, ks, y_hi, y_lo, (e % 2) * EK + at, e % 2 == 0 and at == 0, False,
                       (yl_ready, 0) if e < 2 else None, at=at, done=(at + ks == EK))

            for s in range(12):
                mix(HEADS - 1, s)
                if s in (0, 4, 8):
                    pe.wait_ge(evac_done, NJ * (HEADS - 1) + 5 + s // 4)
                early_blocks(s // 2, 4 * (s % 2), 3 if s % 2 else 4)
            for e in (6, 7):
                early_blocks(e, 0, EK)

            for m in range(ET):
                if m % 2 == 0:
                    pe.wait_ge(lo_ready, U_FIN + m // 2 + 1)
                blocks(early[m][:], m // 2, 2, y_hi, y_lo, KT - 2, False, True, (yl_ready, 0),
                       at=2 * (m % 2), done=(m % 2 == 1))

            def out_units(m, b):
                for u in range(2):
                    pe.wait_ge(lo_ready, U_REST + 2 * (m - ET) + u + 1)
                    blocks(pt[b][:], u, UK, y_hi, y_lo, u * UK, u == 0, u == 1)

            for m in (ET, ET + 1):
                pe.wait_ge(h_final, m - ET + 1)
                out_units(m, m % 2)
            with pe.Fori(ET // 2 + 1, KT // 2) as i:
                for b in range(2):
                    pe.wait_ge(h_final, 2 * i + b - 1)
                    out_units(2 * i + b, b)

            def up_pair(g, i, first=False, waits=None):
                n = U_FFN + U_GRP * g + 4 * i
                for b in range(2):
                    if waits:
                        waits(b)
                    elif b == 0:
                        pe.wait_ge(cg_step, 4 * (FG * g + i - 1) + 1)
                    else:
                        pe.wait_ge(cv_step, 5 * (FG * g + i - 1) + 1)
                    for u in range(2):
                        pe.wait_ge(lo_ready, n + 2 * b + u + 1)
                        blocks(pt[b][:], u, UK, n_hi, n_lo, u * UK, u == 0, u == 1,
                               (nl_ready, KT) if first and b == 0 else None)
                    if first and b == 0:
                        norm_sum(1)

            def down(g, last):
                n = U_FFN + U_GRP * g + 4 * FG
                for m in range(2):
                    pe.wait_ge(lo_ready, n + m + 1)
                    pe.wait_ge(*((cg_step, 4 * (FG * g + FG - 1) + 1) if m == 0 else (cv_step, 5 * (FG * g + FG - 1) + 1)))
                    blocks(pt[m][:], m, FG, f_hi, f_lo, 0, True, True,
                           (fl_ready, FG * g) if m == 0 else None)
                with pe.Fori(1, KT // 2) as i:
                    for b in range(2):
                        m = 2 * i + b
                        pe.wait_ge(lo_ready, n + m + 1)
                        if last:
                            pe.wait_ge(h_final, KT + m - 1)
                        else:
                            pe.wait_ge(down_read, KT * g + m - 1)
                        blocks(pt[b][:], b, FG, f_hi, f_lo, 0, True, True)

            up_pair(0, 0, True, lambda b: pe.wait_ge(h_final, KT - 1 + b))
            with pe.Fori(1, FG) as i:
                up_pair(0, i)
            down(0, False)
            with pe.Fori(1, GROUPS - 1) as g:
                up_pair(g, 0, False, lambda b: pe.wait_ge(down_read, KT * g - 1 + b))
                with pe.Fori(1, FG) as i:
                    up_pair(g, i)
                down(g, False)
            up_pair(GROUPS - 1, 0, False, lambda b: pe.wait_ge(down_read, KT * (GROUPS - 1) - 1 + b))
            with pe.Fori(1, FG) as i:
                up_pair(GROUPS - 1, i)
            down(GROUPS - 1, True)

            def gate_units(m, b, first=False):
                pe.wait_ge(h_final, 2 * KT + m - 1)
                pe.wait_ge(lo_ready, U_PLE + 2 * m + 1)
                ready = (nl_ready, 2 * KT) if first else None
                blocks(pt[b][:], 0, GK, n_hi, n_lo, 0, True, False, ready)
                pe.wait_ge(lo_ready, U_PLE + 2 * m + 2)
                blocks(pt[b][:], 1, KT - GK, n_hi, n_lo, GK, False, True, ready, done=False)
                if first:
                    norm_sum(2)
                    pe.wait_ge(pl_ready, 1)
                blocks(pl[b][:], 1, PK, p_hi, p_lo, 0, True, True, at=KT - GK)

            gate_units(0, 0, True)
            gate_units(1, 1)
            with pe.Fori(1, KT // 2) as i:
                for b in range(2):
                    gate_units(2 * i + b, b)
            norm_sum(3)


def kernel(x, p, norm_mix, w_in, lb_logits, hg_norm, rel_bias, w_out, norm_ffn,
           w_up, conv_w, conv_b, w_down, norm_ple, w_ple_gate, w_ple_proj, final_norm):
    import numpy as np
    import concourse.bacc as bacc
    from concourse.bass_utils import run_bass_kernel_spmd as run

    f32 = [np.asarray(a) for a in (x, p, norm_mix, w_in, lb_logits, hg_norm, rel_bias, w_out, norm_ffn,
                                   w_up, conv_w, conv_b, w_down, norm_ple, w_ple_gate, w_ple_proj, final_norm)]
    (x, p, norm_mix, w_in, lb_logits, hg_norm, rel_bias, w_out, norm_ffn,
     w_up, conv_w, conv_b, w_down, norm_ple, w_ple_gate, w_ple_proj, final_norm) = f32
    c = np.ascontiguousarray

    def units(w, kt):
        rows, cols = w.shape
        g = rows // (P * kt)
        return w.reshape(g, kt, P, cols // P, P).transpose(3, 0, 2, 1, 4).reshape(cols // P, g, P, kt * P)

    order = np.array([part * HEADS + hd for hd in range(HEADS) for part in (1, 0, 2, 3, 4, 5, 6)])
    win = units(w_in[0], UK)[order].reshape(U_OUT, P, UK * P)
    rows = w_out[0].reshape(2, HEADS, P, D).transpose(1, 0, 2, 3).reshape(D, D)
    wout = units(rows[:, ET * P:], UK).reshape(2 * (KT - ET), P, UK * P)
    wearly = units(rows[:2 * EK * P, :ET * P], EK).reshape(2 * ET, P, EK * P)
    wfinish = units(rows[2 * EK * P:, :ET * P], 2)[:, 0].transpose(1, 0, 2).reshape(P, 2 * ET * P)
    up_order = np.array([part * FFT + t for t in range(FFT) for part in (0, 1)])
    wup = units(w_up[0], UK)[up_order].reshape(4 * FFT, P, UK * P)
    wdown = units(w_down[0], FG).transpose(1, 0, 2, 3).reshape(GROUPS * KT, P, FG * P)
    wgate = units(np.concatenate([w_ple_gate[0], w_ple_proj[0]], axis=0), GK).reshape(2 * KT, P, GK * P)
    cv = np.concatenate([conv_w[0], conv_b], axis=0).reshape(4, 2 * FFT, P)[:, up_order].transpose(2, 1, 0)
    gains = np.concatenate([norm_mix, norm_ffn, norm_ple, final_norm[None]], axis=0).reshape(4, KT, P).transpose(2, 0, 1)
    lbt = lb_logits.reshape(2, HEADS, P).transpose(2, 0, 1)
    rel = np.minimum(2 * P, P + P + np.arange(P)[:, None] - np.arange(2 * P)[None, :])
    brow = rel_bias[0].T[rel].transpose(0, 2, 1)
    s, t = np.arange(P)[:, None], np.arange(P)[None, :]
    lv = [s == t] + [(s // (2 * m) == t // (2 * m)) & (s // m % 2 == 0) & (t // m % 2 == 1)
                     for m in (1, 2, 4, 8, 16, 32, 64)]
    lv = [lv[0]] + [b.reshape(P, -1, 2, m)[:, :, 1].reshape(P, P // 2)
                    for b, m in zip(lv[1:], (1, 2, 4, 8, 16, 32, 64))]
    masks = np.concatenate(lv, axis=1).astype(np.float32)
    ins = {
        "in_x": x[0].reshape(S, KT, P).transpose(2, 1, 0), "in_gains": gains, "in_w_in": win,
        "in_lb": lbt, "in_hgn": hg_norm.reshape(P, 1), "in_bias": brow, "in_w_early": wearly,
        "in_w_finish": wfinish, "in_w_out": wout, "in_w_up": wup, "in_conv": cv, "in_w_down": wdown,
        "in_w_gate": wgate,
        "in_p": p[0, 0].reshape(S, PK, P).transpose(2, 1, 0), "in_masks": masks,
        "in_eye": np.eye(P, dtype=np.float32),
    }
    ins = {n: c(a) for n, a in ins.items()}
    nc = bacc.Bacc("TRN2", target_bir_lowering=False, num_devices=1)
    args = [nc.dram_tensor(n, a.shape, mybir.dt.from_np(a.dtype), kind="ExternalInput").ap() for n, a in ins.items()]
    out = nc.dram_tensor("out_t", (P, KT, S), F32, kind="ExternalOutput").ap()
    build(nc, *args, out)
    r = run(nc, [ins], core_ids=[0])
    return c(r.results[0]["out_t"].transpose(2, 1, 0).reshape(1, S, D))
```
